# Optimizing a Trainium2 kernel written in Bass

```python
import jax
import jax.numpy as jnp
from jax import lax
import numpy as np

D_MODEL = 1024
BATCH = 1
SEQ = 1024
DEPTH = 2

CTX_LEN = 256
GRID_W = 64
N_MIXERS = 2
EPS = 1e-6
N_MOD = 6
POOL_WINDOWS = (2, 4, 8, 16)
POOL_GROUPS = 4
POOL_GROUP_DIM = D_MODEL // POOL_GROUPS
MLSTM_HEADS = 8
MLSTM_V_DIM = D_MODEL // MLSTM_HEADS
MLSTM_QK_DIM = MLSTM_V_DIM // 2
MLSTM_QK_WIDTH = MLSTM_HEADS * MLSTM_QK_DIM
MLSTM_V_WIDTH = MLSTM_HEADS * MLSTM_V_DIM
MLSTM_IN_WIDTH = 2 * MLSTM_QK_WIDTH + 2 * MLSTM_V_WIDTH + 4 * MLSTM_HEADS
MLSTM_CHUNK = 64
D_FF = ((8 * D_MODEL // 3 + 255) // 256) * 256
CONV_K = 3
N_POOL_LAYERS = (DEPTH + 1) // 2
N_MLSTM_LAYERS = DEPTH // 2

kernel_name = 'hybrid_pool_mlstm_dit_block'

def _rms_norm(x, g):
    xf = x.astype(jnp.float32)
    y = xf * lax.rsqrt(jnp.mean(xf * xf, axis=-1, keepdims=True) + EPS)
    return (y * g.astype(jnp.float32)).astype(x.dtype)

def _modulation(cond, w, b):
    m = jax.nn.silu(cond) @ w + b
    return jnp.split(m[:, None, :], N_MOD, axis=-1)

def _modulate(h, g, shift, scale):
    return _rms_norm(h, g) * (1 + scale) + shift

def _dwconv_grid(x, w, b, grid):
    B, N, F = x.shape
    R, W = grid
    y = lax.conv_general_dilated(x.reshape(B, R, W, F), w.astype(x.dtype), (1, 1), 'SAME',
                                 dimension_numbers=('NHWC', 'HWIO', 'NHWC'), feature_group_count=F)
    return y.reshape(B, N, F) + b

def _pool_mixer(h, w_groups, scale, grid):
    B, N, D = h.shape
    R, W = grid
    hf = h.astype(jnp.float32).reshape(B, R, W, POOL_GROUPS, POOL_GROUP_DIM)
    csum = jnp.cumsum(hf, axis=2)
    csum = jnp.pad(csum, ((0, 0), (0, 0), (1, 0), (0, 0), (0, 0)))
    pos = np.arange(W)
    outs = []
    for gi, win in enumerate(POOL_WINDOWS):
        lo = np.clip(pos - win // 2, 0, W)
        hi = np.clip(pos - win // 2 + win, 0, W)
        inv_cnt = (1.0 / (hi - lo)).astype(np.float32)[:, None]
        cg = csum[:, :, :, gi]
        mean = (jnp.take(cg, hi, axis=2) - jnp.take(cg, lo, axis=2)) * inv_cnt
        outs.append(mean - hf[:, :, :, gi])
    y = jnp.stack(outs, axis=3).astype(h.dtype)
    y = jnp.einsum('brwgi,gio->brwgo', y, w_groups)
    return y.reshape(B, N, D) * scale

def _mlstm_inputs(h, w_in, b_gate, conv_w, conv_b, grid):
    B, N, _ = h.shape
    z = h @ w_in
    qk, v, o, gates = jnp.split(z, [2 * MLSTM_QK_WIDTH, 2 * MLSTM_QK_WIDTH + MLSTM_V_WIDTH,
                                    2 * MLSTM_QK_WIDTH + 2 * MLSTM_V_WIDTH], axis=-1)
    qk = jax.nn.silu(_dwconv_grid(qk, conv_w, conv_b, grid))
    q, k = jnp.split(qk, 2, axis=-1)

    def heads(a, d):
        return a.reshape(B, N, MLSTM_HEADS, d).transpose(0, 2, 1, 3).astype(jnp.float32)

    q = heads(q, MLSTM_QK_DIM)
    k = heads(k, MLSTM_QK_DIM) * (MLSTM_QK_DIM ** -0.5)
    v = heads(v, MLSTM_V_DIM)
    gates = (gates + b_gate).astype(jnp.float32).reshape(B, N, 4, MLSTM_HEADS).transpose(2, 0, 3, 1)
    return (q, k, v, o, gates[0], gates[1],
            jax.nn.log_sigmoid(gates[2]), jax.nn.log_sigmoid(gates[3]))

def _mlstm_chunkwise(q, k, v, ig, lf, state0, with_output):
    B, H, T, dk = q.shape
    dv = v.shape[-1]
    L = MLSTM_CHUNK
    nc = T // L
    q = q.reshape(B, H, nc, L, dk)
    k = k.reshape(B, H, nc, L, dk)
    v = v.reshape(B, H, nc, L, dv)
    ig = ig.reshape(B, H, nc, L)
    b = jnp.cumsum(lf.reshape(B, H, nc, L), axis=-1)
    b_last = b[..., -1]
    g = b_last[..., None] - b + ig
    g_max = jnp.max(g, axis=-1)
    w_end = jnp.exp(g - g_max[..., None])
    c_chunk = jnp.einsum('bhcsk,bhcsv,bhcs->bhckv', k, v, w_end)
    n_chunk = jnp.einsum('bhcsk,bhcs->bhck', k, w_end)

    def step(carry, xs):
        C, n, m = carry
        bl, gm, cc, ncnk = xs
        m_new = jnp.maximum(bl + m, gm)
        a = jnp.exp(bl + m - m_new)
        e = jnp.exp(gm - m_new)
        C_new = a[..., None, None] * C + e[..., None, None] * cc
        n_new = a[..., None] * n + e[..., None] * ncnk
        return (C_new, n_new, m_new), (C, n, m)

    xs = (jnp.moveaxis(b_last, -1, 0), jnp.moveaxis(g_max, -1, 0),
          jnp.moveaxis(c_chunk, 2, 0), jnp.moveaxis(n_chunk, 2, 0))
    state_f, (c_prev, n_prev, m_prev) = lax.scan(step, state0, xs)
    if not with_output:
        return None, state_f
    c_prev = jnp.moveaxis(c_prev, 0, 2)
    n_prev = jnp.moveaxis(n_prev, 0, 2)
    m_prev = jnp.moveaxis(m_prev, 0, -1)
    mask = np.tril(np.ones((L, L), dtype=bool))
    log_d = jnp.where(mask, b[..., :, None] - b[..., None, :] + ig[..., None, :], -jnp.inf)
    inter_log = b + m_prev[..., None]
    m_t = jnp.maximum(inter_log, jnp.max(log_d, axis=-1))
    d_w = jnp.exp(log_d - m_t[..., None])
    a_t = jnp.exp(inter_log - m_t)
    s = jnp.einsum('bhctk,bhcsk->bhcts', q, k) * d_w
    num = jnp.einsum('bhcts,bhcsv->bhctv', s, v) + a_t[..., None] * jnp.einsum('bhctk,bhckv->bhctv', q, c_prev)
    den = jnp.sum(s, axis=-1) + a_t * jnp.einsum('bhctk,bhck->bhct', q, n_prev)
    h = num / jnp.maximum(jnp.abs(den), jnp.exp(-m_t))[..., None]
    return h.reshape(B, H, T, dv), state_f

def _mlstm_mixer(h, w_in, b_gate, conv_w, conv_b, w_out, grid, state_f0, state_b0, with_output):
    q, k, v, o, ig_f, ig_b, lf_f, lf_b = _mlstm_inputs(h, w_in, b_gate, conv_w, conv_b, grid)
    h_f, st_f = _mlstm_chunkwise(q, k, v, ig_f, lf_f, state_f0, with_output)
    flip = lambda a: jnp.flip(a, axis=2)
    h_b, st_b = _mlstm_chunkwise(flip(q), flip(k), flip(v), flip(ig_b), flip(lf_b), state_b0, with_output)
    if not with_output:
        return None, st_f, st_b
    hs = h_f + flip(h_b)
    B, H, N, dv = hs.shape
    hs = hs.transpose(0, 2, 1, 3).reshape(B, N, H * dv).astype(h.dtype)
    return (jax.nn.sigmoid(o) * hs) @ w_out, st_f, st_b

def _zero_state(batch):
    return (jnp.zeros((batch, MLSTM_HEADS, MLSTM_QK_DIM, MLSTM_V_DIM), jnp.float32),
            jnp.zeros((batch, MLSTM_HEADS, MLSTM_QK_DIM), jnp.float32),
            jnp.zeros((batch, MLSTM_HEADS), jnp.float32))

def _conv_ffn(h, w_in, conv_w, conv_b, w_out, grid):
    u, g = jnp.split(h @ w_in, 2, axis=-1)
    g = _dwconv_grid(g, conv_w, conv_b, grid)
    return (jax.nn.silu(g) * u) @ w_out

def setup_inputs(seed: int = 0) -> dict:
    key = jax.random.key(seed)
    ks = jax.random.split(key, 20)
    nrm = jax.random.normal
    f32 = jnp.float32
    b_gate = jnp.concatenate([0.1 * nrm(ks[10], (N_MLSTM_LAYERS, 2 * MLSTM_HEADS), f32),
                              3.0 + 0.5 * nrm(ks[11], (N_MLSTM_LAYERS, 2 * MLSTM_HEADS), f32)], axis=-1)
    return {
        'x': nrm(ks[0], (BATCH, SEQ, D_MODEL), f32),
        'c': nrm(ks[1], (BATCH, D_MODEL), f32),
        'ctx': nrm(ks[2], (BATCH, CTX_LEN, D_MODEL), f32),
        'c_ctx': nrm(ks[3], (D_MODEL,), f32),
        'mod_w': nrm(ks[4], (DEPTH, D_MODEL, N_MOD * D_MODEL), f32) * D_MODEL ** -0.5,
        'mod_b': 0.02 * nrm(ks[5], (DEPTH, N_MOD * D_MODEL), f32),
        'norm_g': 1.0 + 0.05 * nrm(ks[6], (DEPTH, 4, D_MODEL), f32),
        'pool_w': nrm(ks[7], (N_POOL_LAYERS, POOL_GROUPS, POOL_GROUP_DIM, POOL_GROUP_DIM), f32) * POOL_GROUP_DIM ** -0.5,
        'pool_scale': 1.0 + 0.05 * nrm(ks[8], (N_POOL_LAYERS, D_MODEL), f32),
        'mlstm_w_in': nrm(ks[9], (N_MLSTM_LAYERS, D_MODEL, MLSTM_IN_WIDTH), f32) * D_MODEL ** -0.5,
        'mlstm_b_gate': b_gate,
        'mlstm_conv_w': nrm(ks[12], (N_MLSTM_LAYERS, CONV_K, CONV_K, 1, 2 * MLSTM_QK_WIDTH), f32) / CONV_K,
        'mlstm_conv_b': 0.02 * nrm(ks[13], (N_MLSTM_LAYERS, 2 * MLSTM_QK_WIDTH), f32),
        'mlstm_w_out': nrm(ks[14], (N_MLSTM_LAYERS, MLSTM_V_WIDTH, D_MODEL), f32) * MLSTM_V_WIDTH ** -0.5,
        'ffn_w_in': nrm(ks[15], (DEPTH, D_MODEL, 2 * D_FF), f32) * D_MODEL ** -0.5,
        'ffn_conv_w': nrm(ks[16], (DEPTH, CONV_K, CONV_K, 1, D_FF), f32) / CONV_K,
        'ffn_conv_b': 0.02 * nrm(ks[17], (DEPTH, D_FF), f32),
        'ffn_w_out': nrm(ks[18], (DEPTH, D_FF, D_MODEL), f32) * D_FF ** -0.5,
    }

def reference(x, c, ctx, c_ctx, mod_w, mod_b, norm_g, pool_w, pool_scale, mlstm_w_in, mlstm_b_gate,
              mlstm_conv_w, mlstm_conv_b, mlstm_w_out, ffn_w_in, ffn_conv_w, ffn_conv_b, ffn_w_out):
    B, N, _ = x.shape
    ROWS = N // GRID_W
    grid_x = (ROWS, GRID_W)
    grid_c = (1, ctx.shape[1])
    for i in range(DEPTH):
        last = i == DEPTH - 1
        j = i // N_MIXERS
        use_pool = i % N_MIXERS == 0
        ctx_out = not last
        ctx_read = ctx_out or not use_pool
        sh1, sc1, gt1, sh2, sc2, gt2 = _modulation(c, mod_w[i], mod_b[i])
        hx = _modulate(x, norm_g[i, 0], sh1, sc1)
        if ctx_read:
            csh1, csc1, cgt1, csh2, csc2, cgt2 = _modulation(c_ctx[None, :], mod_w[i], mod_b[i])
            hc = _modulate(ctx, norm_g[i, 0], csh1, csc1)
        if use_pool:
            yx = _pool_mixer(hx, pool_w[j], pool_scale[j], grid_x)
            yc = _pool_mixer(hc, pool_w[j], pool_scale[j], grid_c) if ctx_out else None
        else:
            z0 = _zero_state(B)
            yc, st_f, st_b = _mlstm_mixer(hc, mlstm_w_in[j], mlstm_b_gate[j], mlstm_conv_w[j], mlstm_conv_b[j],
                                          mlstm_w_out[j], grid_c, z0, z0, ctx_out)
            yx, _, _ = _mlstm_mixer(hx, mlstm_w_in[j], mlstm_b_gate[j], mlstm_conv_w[j], mlstm_conv_b[j],
                                    mlstm_w_out[j], grid_x, st_f, st_b, True)
        x = x + gt1 * _rms_norm(yx, norm_g[i, 1])
        fx = _conv_ffn(_modulate(x, norm_g[i, 2], sh2, sc2), ffn_w_in[i], ffn_conv_w[i], ffn_conv_b[i], ffn_w_out[i], grid_x)
        x = x + gt2 * _rms_norm(fx, norm_g[i, 3])
        if ctx_out:
            ctx = ctx + cgt1 * _rms_norm(yc, norm_g[i, 1])
            fc = _conv_ffn(_modulate(ctx, norm_g[i, 2], csh2, csc2), ffn_w_in[i], ffn_conv_w[i], ffn_conv_b[i], ffn_w_out[i], grid_c)
            ctx = ctx + cgt2 * _rms_norm(fc, norm_g[i, 3])
    return x


_drawn_inputs = setup_inputs


def setup_inputs(seed=0):
    import zlib

    import numpy as np

    out = dict(_drawn_inputs(seed))
    spreads = {}
    factors = {'ctx': 2.817, 'mlstm_conv_b': 5.006, 'ffn_conv_b': 5.22}
    for name, (base, spread) in spreads.items():
        noise = np.random.default_rng([zlib.crc32(name.encode()), seed]).standard_normal(out[name].shape)
        drawn = base * np.exp(spread * noise) if base else spread * noise
        out[name] = jnp.asarray(drawn.astype(out[name].dtype))
    for name, factor in factors.items():
        out[name] = (out[name] * factor).astype(out[name].dtype)
    return out
```

```python
from contextlib import ExitStack

import numpy as np

import concourse.bass as bass
from concourse import mybir

F32 = mybir.dt.float32
F32R = mybir.dt.float32r
ALU = mybir.AluOpType
ACT = mybir.ActivationFunctionType

P = 128
D = 1024
KT = D // P
TX = 1024
TC = 256
GRID = {"x": (16, 64), "c": (1, 256)}
TOK = {"x": TX, "c": TC}
DFF = 2816
FT = DFF // P
HEADS = 8
CH = 128
NCH = (TX + TC) // CH
EPS = 1e-6
WINDOWS = (2, 4, 8, 16)
PAD = 8
WT = 3072
CREDIT = 2
MASKED = -1e30

K_FFN0, K_FFNC, K_MIN, K_GATE, K_MOUT = 0, FT, 2 * FT, 2 * FT + 8, 2 * FT + 9
K_FFN1 = K_MOUT + 3
PM_MODB, PM_G, PM_PS, PM_MCV, PM_GB, PM_EPS = 0, 96, 160, 168, 248, 249
N_PRM = 250


class Pass:

    def __init__(self, index, stream, layer, k0, y0, tap0):
        self.index, self.stream, self.layer = index, stream, layer
        self.T = TOK[stream]
        self.R, self.W = GRID[stream]
        self.chunks = max(1, self.T // 512)
        self.cw = self.T // self.chunks
        self.j0 = index * FT
        self.k0 = k0
        self.y0 = y0
        self.tap0 = tap0
        self.taps = taps_of(stream)


def taps_of(stream):
    rows = (-1, 0, 1) if GRID[stream][0] > 1 else (0,)
    return [(r, c) for r in rows for c in (-1, 0, 1) if (r, c) != (0, 0)]


def tap_index(r, c):
    return 3 * (r + 1) + c + 1


def tap_views(dst, src, r, c, R, W):
    r0, r1 = max(0, -r), min(R, R - r)
    c0, c1 = max(0, -c), min(W, W - c)
    return dst[:, r0:r1, c0:c1], src[:, r0 + r:r1 + r, c0 + c:c1 + c]


PASSES = [Pass(0, "x", 0, K_FFN0, 0, 0),
          Pass(1, "c", 0, K_FFNC, FT, 8 * FT),
          Pass(2, "x", 1, K_FFN1, 2 * FT + 3, 8 * FT + 2 * FT)]


def build(nc, a):
    with ExitStack() as ctx:
        sems = {}

        def sem(name):
            if name not in sems:
                sems[name] = ctx.enter_context(nc.semaphore(name))
            return sems[name]

        base = (nc.sbuf_base + 63) // 64 * 64

        def at(name, offset, shape, dt=F32):
            return nc.alloc_sbuf_tensor_at(name, shape, dt, offset=base + offset)

        H_HI, H_LO, Y_AT, RAW, W_HI, W_LO, WORK = 0, 32768, 65536, 98304, 122880, 147456, 172032
        SMALL = WORK + 32768

        hx_hi = at("hx_hi", H_HI, [P, KT, TX], F32R)
        hx_lo = at("hx_lo", H_LO, [P, KT, TX], F32R)
        y_x = at("y_x", Y_AT, [P, KT, TX])
        mix_in_x = at("mix_in_x", H_HI, [P, KT, TX])
        mix_out_x = at("mix_out_x", H_LO, [P, KT, TX])
        res_x = at("res_x", H_HI, [P, KT, TX])
        hc_hi = at("hc_hi", H_LO, [P, KT, TC], F32R)
        hc_lo = at("hc_lo", H_LO + 8192, [P, KT, TC], F32R)
        y_c = at("y_c", H_LO + 16384, [P, KT, TC])
        res_c = at("res_c", H_LO + 24576, [P, KT, TC])
        raw = at("raw", RAW, [P, 2, WT])
        w_hi = at("w_hi", W_HI, [P, 2, WT], F32R)
        w_lo = at("w_lo", W_LO, [P, 2, WT], F32R)
        modw = at("modw", RAW, [P, 4, 2048])
        in_c = at("in_c", W_HI + 8192, [P, KT, TC])
        mix_in_c = at("mix_in_c", W_HI + 16384, [P, KT, TC])
        mix_out_c = at("mix_out_c", W_LO, [P, KT, TC])
        pool_w = at("pool_w", W_LO + 8192, [P, 4, 2, 256])
        inv_x = at("inv_x", W_LO + 16384, [P, 4, 64])
        inv_c = at("inv_c", W_LO + 16384 + 1024, [P, 4, 256])
        modrow = at("modrow", W_LO + 21504, [P, 512])
        acc = at("acc", WORK, [P, TX])
        prod = at("prod", WORK + 4096, [P, TX])
        a_hi = at("a_hi", WORK + 8192, [P, 2, TX], F32R)
        a_lo = at("a_lo", WORK + 16384, [P, 2, TX], F32R)
        sq = at("sq", WORK, [P, 2, TX])
        zpad = at("zpad", WORK + 8192, [P, 1280])
        sum_a = at("sum_a", WORK + 13312, [P, 1280])
        sum_b = at("sum_b", WORK + 18432, [P, 1280])
        rstd = [at("rstd0", WORK + 24576, [P, TX]), at("rstd1", WORK + 28672, [P, TX])]
        q_x = at("q_x", Y_AT, [P, 4, TX])
        k_x = at("k_x", Y_AT + 16384, [P, 4, TX])
        acc_c = at("acc_c", WORK + 4096, [P, TC])
        mc_hi = at("mc_hi", WORK + 8192, [P, KT, TC], F32R)
        mc_lo = at("mc_lo", WORK + 16384, [P, KT, TC], F32R)
        k_c = at("k_c", WORK + 24576, [P, 4, TC])
        stage = at("stage", WORK + 28672, [P, 2, 384])
        NT = NCH * CH
        gates = at("gates", WORK, [P, NT])
        gtmp = at("gtmp", WORK + 5120, [P, NT])
        logf = at("logf", WORK + 10240, [P, NT])
        gcum = at("gcum", WORK + 15360, [P, NT])
        GA = W_HI
        gmax = at("gmax", GA, [P, NT])
        gr = at("gr", GA + 5120, [P, NT])
        gc_ = at("gc", GA + 10240, [P, NT])
        gw = at("gw", GA + 15360, [P, NT])
        ga = at("ga", GA + 20480, [P, NT])
        gem = at("gem", GA + 25600, [P, NT])
        greset = at("greset", GA + 30720, [P, NT])
        cols = at("cols", GA + 41088, [P, NCH, 3, 64])
        alpha = at("alpha", GA + 48768, [P, 2, 4, NCH])
        gend = at("gend", WORK + 20480, [P, 4, NCH])
        dmat = at("dmat", GA, [P, 2, HEADS, CH])
        qa = at("qa", GA + 8192, [P, 2, 4, CH])
        vch = at("vch", GA + 12288, [P, 2, HEADS, P + 1])
        kw = at("kw", GA + 20544, [P, 2, 512])
        state = at("state", GA + 24640, [P, 2, HEADS, P + 1])
        och = at("och", WORK, [P, 1024])
        tmp = at("tmp", WORK + 4096, [P, 2, 1024])
        masks = at("masks", WORK + 12288, [P, 2, CH])
        hs = at("hs", H_LO, [P, 8, 1024])
        g_hi = at("g_hi", H_HI, [P, 8, HEADS, CH], F32R)
        g_lo = at("g_lo", H_LO, [P, 8, HEADS, CH], F32R)
        small = [SMALL]

        def little(name, shape, dt=F32):
            t = at(name, small[0], shape, dt)
            small[0] += (4 * int(np.prod(shape[1:])) + 31) // 32 * 32
            return t

        prm = little("prm", [P, N_PRM])
        fcv = little("fcv", [P, 2 * FT, 10])
        modt = little("modt", [P, 2, 96])
        der = little("der", [P, 2, 2, 4, KT])
        c_in = little("c_in", [P, KT, 2])
        c_pad = little("c_pad", [P, KT, 32])
        ident = little("ident", [P, P])
        ones = little("ones", [P, P])
        dens = little("dens", [P, 3, HEADS])
        assert base + small[0] <= nc.SBUF_PARTITION_SIZE_BYTES
        ps = ctx.enter_context(nc.psum_tensor("ps", [P, 8, 512], F32))

        def scratch(name, shape):
            return nc.dram_tensor(name, shape, F32, kind="Internal").ap()

        x_scr = scratch("x_scr", (2, P, KT, TX))
        xc_scr = scratch("xc_scr", (P, KT, TC))
        hc_scr = scratch("hc_scr", (P, KT, TC))
        v_scr = scratch("v_scr", (NCH, P, 1024))
        o_scr = scratch("o_scr", (8, P, 1024))
        row_scr = scratch("row_scr", (2, 64, NT))
        al_scr = scratch("al_scr", (64, NCH))

        def bank(b0, T):
            v = ps[:, b0:b0 + 2, :].rearrange("p b n -> p (b n)")
            return v[:, 0:T]

        def ssq(T):
            return ps[:, 1:4:2, :] if T == TX else ps[:, 1, 0:T]

        def halves(ap, T):
            return ap.rearrange("p (b n) -> p b n", n=512) if T == TX else ap

        def grid(ap, s):
            return ap.rearrange("p (r w) -> p r w", w=GRID[s][1])

        def mod(layer, sec, s):
            c0 = layer * 48 + sec * 8
            return modt[:, 0 if s == "x" else 1, c0:c0 + 8]

        def derived(layer, which, s, d):
            return der[:, layer, 0 if s == "x" else 1, which, d:d + 1]

        def shift(layer, which, s, d):
            c0 = layer * 48 + 24 * which + d
            return modt[:, 0 if s == "x" else 1, c0:c0 + 1]

        def prmc(c):
            return prm[:, c:c + 1]

        norms = {}
        for n, key in enumerate(["c_in", "x_in", "c_mix", "c_pre2", "x_mix", "x_pre2", "x_ffn0",
                                 "c_ffn", "c_pre1", "x_pre1", "x_mlstm", "x_pre2b", "x_out"]):
            norms[key] = n
        posts = {k: n for n, k in enumerate(["c_mix", "x_mix", "x_ffn0", "c_ffn", "x_mlstm", "x_out"])}
        pres = {k: n for n, k in enumerate(["c_pre2", "x_pre2", "c_pre1", "x_pre1", "x_pre2b"])}

        splits = {k: n for n, k in enumerate(["x_pre2", "c_pre1", "x_pre1", "x_pre2b"])}

        order_b = [1, 0] + list(range(NCH - 1, 1, -1))
        units = []
        for s in range(NCH):
            units += [(0, s), (1, order_b[s])]
        x_units = [u for u, (_, n) in enumerate(units) if n >= 2]
        x_index = {u: i for i, u in enumerate(x_units)}
        seen, second = set(), []
        for u in x_units:
            n = units[u][1]
            if n in seen:
                second.append(u)
            seen.add(n)
        sec_index = {u: i for i, u in enumerate(second)}
        evacs = []
        for t in range(8):
            m0 = max(3 * t, 8)
            w = (3 * t + 3 - m0) * P
            if w <= 0:
                continue
            for n in range(NCH):
                cw = w if n >= 2 else max(0, min(16, 3 * t + 3) - m0) * P
                if cw:
                    evacs.append((t, n, m0, cw))
        stage_total = []
        run = [0, 0]
        for e, (t, n, m0, w) in enumerate(evacs):
            both = m0 < 16 < m0 + w // P
            run[e % 2] += 32 if both else 16
            stage_total.append(run[e % 2])

        def in_use(K):
            if K < 0:
                return []
            if K < K_MIN:
                return [("w_in_used", K + 1 + CREDIT), ("w_out_used", K + 1 + CREDIT)]
            t = K - K_MIN
            if t < 8:
                got = [("qk_done", 3)] if t == 0 else [("kc_done", 2)] if t == 1 else \
                    [("vo_done", sum(1 for ev in evacs if ev[0] <= t))]
                return got + ([("unit_done", len(units)), ("state_ready", 8 * len(units))] if t == 7 else [])
            return [("gates_done", 1)] if K == K_GATE else [("mo_part", 8 * (K - K_MOUT + 1))]

        block = ctx.enter_context(nc.Block())

        @block.sync
        def _(sp):
            for dst, src in ((c_in, a["ccol"]), (prm, a["prm"]), (fcv, a["fcv"]), (ident, a["ident"]),
                             (inv_x, a["inv_x"]), (inv_c, a["inv_c"]), (pool_w, a["pool_w"])):
                sp.dma_start(dst[:], src).then_inc(sem("const_in"), 16)
            sp.dma_start(in_c[:], a["ctx"]).then_inc(sem("ctx_in"), 16)
            sp.dma_start(y_x[:], a["x"]).then_inc(sem("x_in"), 16)
            for q in range(48):
                if q >= 4:
                    sp.wait_ge(sem("modw_used"), q - 3)
                sp.dma_start(modw[:, q % 4, :], a["modw"][q]).then_inc(sem(f"modw_in{q % 4}"), 16)

            def tile(K, src, slot):
                sp.wait_ge(sem("lo_in"), K + 1)
                sp.wait_ge(sem("lo_out"), K + 1)
                sp.dma_start(raw[:, slot, :], src).then_inc(sem(f"raw_in{slot}"), 16)

            def first_two(p):
                for j in range(2):
                    tile(p.k0 + j, a["ffn_w"][p.layer * FT + j], (p.k0 + j) % 2)

            def the_rest(p):
                with sp.Fori(0, FT // 2 - 1) as i:
                    for e in range(2):
                        tile(i * 2 + (p.k0 + 2 + e), a["ffn_w"][i * 2 + (p.layer * FT + 2 + e)], (p.k0 + e) % 2)

            p0, p1, p2 = PASSES
            sp.wait_ge(sem("modw_used"), 48)
            first_two(p0)
            the_rest(p0)
            first_two(p1)
            sp.wait_ge(sem("w_in_used"), FT + CREDIT)
            sp.wait_ge(sem("x_out"), 16 * KT)
            sp.dma_start(res_x[:], x_scr[0]).then_inc(sem("res_in"), 16)
            sp.wait_ge(sem("hc_out"), 16)
            sp.dma_start(res_c[:], hc_scr).then_inc(sem("hc_in"), 16)
            the_rest(p1)
            sp.wait_ge(sem("hc_split"), 8)
            sp.wait_ge(sem("xc_out"), 16 * KT)
            sp.dma_start(res_c[:], xc_scr).then_inc(sem("resc_in"), 16)
            for t in range(12):
                K = K_MIN + t
                tile(K, a["mlstm_w"][t], K % 2)
                if K == K_GATE:
                    sp.wait_ge(sem("rows_ready"), 3)
                    for n, src in enumerate((gr, ga)):
                        sp.dma_start(row_scr[n], src[0:64, :]).then_inc(sem("rows_out"), 16)
                    sp.dma_start(al_scr, gend[0:64, 3, :]).then_inc(sem("rows_out"), 16)
                    sp.wait_ge(sem("rows_out"), 48)
                    for dr in range(2):
                        for par in range(2):
                            src = al_scr[32 * dr + par:32 * dr + 8:2, :]
                            sp.dma_start(alpha[64 * par:64 * par + 64, dr], src.unsqueeze(0).broadcast_to([64, 4, NCH]))\
                                .then_inc(sem("alpha_in"), 16)
                    sp.dma_start(masks[:], a["masks"]).then_inc(sem("mask_in"), 16)
                    sp.wait_ge(sem("cols_ready"), 4)
                    sp.wait_ge(sem("state_zero"), 2)
                    for i in range(2):
                        sp.wait_ge(sem(f"stage_out{i}"), run[i])
                    for u, (dr, n) in enumerate(units):
                        if u >= 2:
                            sp.wait_ge(sem("unit_done"), u - 1)
                        sp.dma_start(vch[:, u % 2, :, 0:P], v_scr[n].rearrange("p (h v) -> p h v", v=P))\
                            .then_inc(sem(f"v_in{u % 2}"), 16)
                        if n >= 2:
                            for par in range(2):
                                rows = slice(32 * dr + par, 32 * dr + 8, 2)
                                src = row_scr[0, rows, n * CH:n * CH + CH]
                                sp.dma_start(dmat[:, u % 2, 4 * par:4 * par + 4, :],
                                             src.unsqueeze(0).broadcast_to([P, 4, CH])).then_inc(sem(f"row_in{u % 2}"), 16)
                                src = row_scr[1, rows, n * CH:n * CH + CH]
                                sp.dma_start(qa[64 * par:64 * par + 64, u % 2],
                                             src.unsqueeze(0).broadcast_to([64, 4, CH])).then_inc(sem(f"row_in{u % 2}"), 16)
                        if u in sec_index:
                            i = sec_index[u]
                            if i >= 1:
                                sp.wait_ge(sem("gated"), i)
                            sp.dma_start(och[:], o_scr[n - 2]).then_inc(sem("o_in"), 16)
            first_two(p2)
            sp.wait_ge(sem("mo_part"), 24)
            sp.wait_ge(sem("x_out"), 32 * KT)
            sp.dma_start(res_x[:], x_scr[1]).then_inc(sem("res_in"), 16)
            the_rest(p2)
            sp.wait_ge(sem("w_in_used"), 3 * FT + CREDIT)
            sp.wait_ge(sem("x_out"), 48 * KT)
            sp.dma_start(res_x[:], x_scr[0]).then_inc(sem("res_in"), 16)
            for d in range(KT):
                sp.wait_ge(sem("post_done"), 8 * posts["x_out"] + d + 1)
                sp.dma_start(a["out"][:, d, :], y_x[:, d, :]).then_inc(sem("out_done"), 16)
            sp.wait_ge(sem("out_done"), 16 * KT)

        @block.tensor
        def _(pe):
            def triple(out, whi, wlo, hhi, hlo, first, last):
                pe.matmul(out, whi, hhi, start=first, stop=False)
                pe.matmul(out, whi, hlo, start=False, stop=False)
                return pe.matmul(out, wlo, hhi, start=False, stop=last)

            def norm(key, T):
                N = norms[key]
                if N >= 1:
                    pe.wait_ge(sem("std_ready"), N)
                for k in range(KT):
                    pe.wait_ge(sem("sq_ready"), 8 * N + k + 1)
                    for c in range(max(1, T // 512)):
                        w = min(512, T)
                        mm = pe.matmul(ps[:, 1 + 2 * c, 0:w], ones[:], sq[:, k % 2, c * w:c * w + w],
                                       start=(k == 0), stop=(k == KT - 1), skip_group_check=True)
                    mm.then_inc(sem("sq_used"), 1)

            def mod_round(r):
                for k in range(KT):
                    q = KT * r + k
                    pe.wait_ge(sem(f"modw_in{q % 4}"), 16 * (q // 4 + 1))
                    for g in range(4):
                        mm = pe.matmul(ps[32 * g:32 * g + 32, 0, :], c_pad[:, k, :], modw[:, q % 4, 512 * g:512 * g + 512],
                                       start=(k == 0), stop=(k == KT - 1), tile_position=(0, 32 * g))
                    mm.then_inc(sem("modw_used"), 1)
                pe.wait_ge(sem("modrow_ready"), r + 1)
                if r >= 1:
                    pe.wait_ge(sem("mod_done"), r)
                for b in range(4):
                    mm = pe.transpose(ps[:, 2, P * b:P * b + P], modrow[:, P * b:P * b + P], ident[:])
                mm.then_inc(sem("modcol_ready"), 1)

            def mixer(s, first):
                T = TOK[s]
                src = mix_in_x if s == "x" else mix_in_c
                w = min(512, T)
                for d in range(KT):
                    g, mo = d // 2, d % 2
                    if mo == 0:
                        pe.wait_ge(sem("mix_in_ready"), first + 2 * g + 2)
                    if first + d >= 2:
                        pe.wait_ge(sem("mix_out_ready"), first + d - 1)
                    for c in range(max(1, T // 512)):
                        for ki in range(2):
                            mm = pe.matmul(ps[:, 4 + 2 * (d % 2) + c, 0:w], pool_w[:, g, ki, P * mo:P * mo + P],
                                           src[:, 2 * g + ki, c * w:c * w + w], start=(ki == 0), stop=(ki == 1))
                    mm.then_inc(sem("mix_done"), 1)

            def ffn(p, h_hi, h_lo, pre_base):
                def project_in(j, par, first=False):
                    s = (p.k0 + par) % 2
                    pe.wait_ge(sem("lo_in"), j + (p.k0 + 1 + CREDIT))
                    for part in range(2):
                        if part == 0:
                            if not (first and p.tap0 == 0):
                                pe.wait_ge(sem("tap_done"), j * len(p.taps) + p.tap0)
                        elif not (first and p.j0 == 0):
                            pe.wait_ge(sem("a_done"), j + p.j0)
                        for c in range(p.chunks):
                            for k in range(KT):
                                if first and part == 0 and c == 0 and pre_base is not None:
                                    pe.wait_ge(sem("pre_lo"), pre_base + k + 1)
                                cs = slice(c * p.cw, c * p.cw + p.cw)
                                ws = slice(1024 * part + P * k, 1024 * part + P * k + P)
                                mm = triple(ps[:, 2 * part + c, 0:p.cw], w_hi[:, s, ws], w_lo[:, s, ws],
                                            h_hi[:, k, cs], h_lo[:, k, cs], k == 0, k == KT - 1)
                        mm.then_inc(sem("g_done" if part == 0 else "w_in_used"), 1)

                def project_out(j, par):
                    s = (p.k0 + par) % 2
                    pe.wait_ge(sem("a_lo_ready"), j + (p.j0 + 1))
                    pe.wait_ge(sem("lo_out"), j + (p.k0 + 1 + CREDIT))
                    for d in range(KT):
                        pe.wait_ge(sem("y_added"), j * 8 + (8 * p.y0 + d + 7))
                        ws = slice(2048 + P * d, 2048 + P * d + P)
                        for c in range(p.chunks):
                            cs = slice(c * p.cw, c * p.cw + p.cw)
                            mm = triple(ps[:, 4 + 2 * (d % 2) + c, 0:p.cw], w_hi[:, s, ws], w_lo[:, s, ws],
                                        a_hi[:, par, cs], a_lo[:, par, cs], True, True)
                        mm.then_inc(sem("y_part" if d < 7 else "w_out_used"), 1)

                project_in(0, 0, True)
                with pe.Fori(0, FT // 2 - 1) as i:
                    project_in(i * 2 + 1, 1)
                    project_out(i * 2, 0)
                    project_in(i * 2 + 2, 0)
                    project_out(i * 2 + 1, 1)
                project_in(FT - 1, 1)
                project_out(FT - 2, 0)
                project_out(FT - 1, 1)

            pe.wait_ge(sem("const_in"), 7 * 16)
            pe.wait_ge(sem("ones_ready"), 1)
            pe.wait_ge(sem("cpad_ready"), 1)
            norm("c_in", TC)
            norm("x_in", TX)
            for r in range(3):
                mod_round(r)
            mixer("c", 0)
            norm("c_mix", TC)
            norm("c_pre2", TC)
            mod_round(3)
            mixer("x", KT)
            norm("x_mix", TX)
            mod_round(4)
            norm("x_pre2", TX)
            mod_round(5)
            p0, p1, p2 = PASSES
            ffn(p0, hx_hi, hx_lo, 8 * splits["x_pre2"])
            norm("x_ffn0", TX)
            pe.wait_ge(sem("hc_split"), 8)
            ffn(p1, hc_hi, hc_lo, None)
            norm("c_ffn", TC)
            norm("c_pre1", TC)
            norm("x_pre1", TX)

            pe.wait_ge(sem("pre_lo"), 8 * splits["c_pre1"] + 8)
            e = 0
            for t in range(8):
                K = K_MIN + t
                s = K % 2
                pe.wait_ge(sem("lo_in"), K + 1 + CREDIT)
                pe.wait_ge(sem("lo_out"), K + 1 + CREDIT)

                def wcol(part, k, m0, n):
                    c0 = 384 * k + P * (m0 - 3 * t)
                    return (w_hi if part == 0 else w_lo)[:, s, c0:c0 + P * n]

                for m in range(3 * t, min(3 * t + 3, 8)):
                    if m >= 2:
                        pe.wait_ge(sem("qtap_done"), 8 * (m - 1))
                    for c in range(2):
                        for k in range(KT):
                            if m == 0 and c == 0:
                                pe.wait_ge(sem("pre_lo"), 8 * splits["x_pre1"] + k + 1)
                            mm = triple(ps[:, 2 * (m % 2) + c, :], wcol(0, k, m, 1), wcol(1, k, m, 1),
                                        hx_hi[:, k, 512 * c:512 * c + 512], hx_lo[:, k, 512 * c:512 * c + 512],
                                        k == 0, k == KT - 1)
                    mm.then_inc(sem("qk_done"), 1)
                    if m >= 4:
                        if m >= 5:
                            pe.wait_ge(sem("kctap_done"), 2 * (m - 4))
                        for k in range(KT):
                            mm = triple(ps[:, 4, 0:TC], wcol(0, k, m, 1), wcol(1, k, m, 1), mc_hi[:, k, :], mc_lo[:, k, :],
                                        k == 0, k == KT - 1)
                        mm.then_inc(sem("kc_done"), 1)
                while e < len(evacs) and evacs[e][0] == t:
                    _, n, m0, w = evacs[e]
                    if e >= 3:
                        pe.wait_ge(sem("stage_ready"), e - 2)
                    hi, lo, t0 = (hx_hi, hx_lo, (n - 2) * CH) if n >= 2 else (mc_hi, mc_lo, n * CH)
                    out = ps[:, 5 + e % 3, 0:w]
                    for k in range(KT):
                        pe.matmul(out, hi[:, k, t0:t0 + CH], wcol(0, k, m0, w // P), start=(k == 0), stop=False)
                        pe.matmul(out, hi[:, k, t0:t0 + CH], wcol(1, k, m0, w // P), start=False, stop=False)
                        mm = pe.matmul(out, lo[:, k, t0:t0 + CH], wcol(0, k, m0, w // P), start=False, stop=(k == KT - 1))
                    mm.then_inc(sem("vo_done"), 1)
                    e += 1
            K, s = K_GATE, K_GATE % 2
            pe.wait_ge(sem("lo_in"), K + 1 + CREDIT)
            pe.wait_ge(sem("qtap_done"), 8 * 8)
            for part, (T, hi, lo) in enumerate(((512, hx_hi, hx_lo), (512, hx_hi, hx_lo), (TC, mc_hi, mc_lo))):
                t0 = 512 if part == 1 else 0
                for k in range(KT):
                    mm = triple(ps[:, part, 0:T], w_hi[:, s, P * k:P * k + P], w_lo[:, s, P * k:P * k + P],
                                hi[:, k, t0:t0 + T], lo[:, k, t0:t0 + T], k == 0, k == KT - 1)
            mm.then_inc(sem("gates_done"), 1)
            pe.wait_ge(sem("gates_ready"), 2)
            for n in range(NCH):
                for i, src in enumerate((gc_, gw, gem)):
                    b = 3 * n + i
                    mm = pe.transpose(ps[:, 4 + b // 8, 64 * (b % 8):64 * (b % 8) + 64], src[0:64, n * CH:n * CH + CH], ident[0:64, 0:64])
            mm.then_inc(sem("gcols_done"), 1)

            def k_tile(n, pair):
                return k_x[:, pair, (n - 2) * CH:(n - 1) * CH] if n >= 2 else k_c[:, pair, n * CH:(n + 1) * CH]

            def front(u):
                dr, n = units[u]
                if u >= 1:
                    pe.wait_ge(sem("kw_ready"), u)
                else:
                    pe.wait_ge(sem("cols_ready"), 4)
                for pair in range(4):
                    mm = pe.transpose(ps[:, 5, P * pair:P * pair + P], k_tile(n, pair), ident[:])
                mm.then_inc(sem("kt_done"), 1)
                if n >= 2:
                    i = x_index[u]
                    done = sum(1 for v in second if v <= u - 3)
                    if i >= 1:
                        pe.wait_ge(sem("sd_ready"), i)
                    if done:
                        pe.wait_ge(sem("glo_ready"), done)
                    for pair in range(4):
                        for par in range(2):
                            r = slice(64 * par, 64 * par + 64)
                            t = slice((n - 2) * CH, (n - 1) * CH)
                            mm = pe.matmul(ps[:, par, P * pair:P * pair + P], k_x[r, pair, t], q_x[r, pair, t],
                                           start=True, stop=True)
                    mm.then_inc(sem("s_done"), 1)

            def back(u):
                dr, n = units[u]
                pe.wait_ge(sem(f"v_in{u % 2}"), 16 * (u // 2 + 1))
                if n >= 2:
                    i = x_index[u]
                    pe.wait_ge(sem("sd_ready"), i + 1)
                    pe.wait_ge(sem("qa_ready"), i + 1)
                    if i >= 1:
                        pe.wait_ge(sem("hs_ready"), i)
                    pe.wait_ge(sem("state_ready"), 8 * (u - 1))
                    for h in range(HEADS):
                        pair, par = h // 2, h % 2
                        out = ps[:, 2 + h // 3, (P + 1) * (h % 3):(P + 1) * (h % 3 + 1)]
                        pe.matmul(out, dmat[:, u % 2, 4 * par + pair, :], vch[:, u % 2, h, :], start=True, stop=False)
                        mm = pe.matmul(out, qa[:, u % 2, pair, :], state[:, dr, h, :], start=False, stop=True)
                    mm.then_inc(sem("num_done"), 1)
                pe.wait_ge(sem("kw_ready"), u + 1)
                if u >= 1:
                    pe.wait_ge(sem("state_ready"), 8 * u)
                for h in range(HEADS):
                    pair, par = h // 2, h % 2
                    out = ps[64 * par:64 * par + 64, 6 + pair // 3, (P + 1) * (pair % 3):(P + 1) * (pair % 3 + 1)]
                    mm = pe.matmul(out, kw[:, u % 2, 64 * h:64 * h + 64], vch[:, u % 2, h, :], start=True, stop=True)
                mm.then_inc(sem("unit_done"), 1)

            def turn(u):
                if u not in sec_index:
                    return
                i = sec_index[u]
                pe.wait_ge(sem("gated"), i + 1)
                pe.wait_ge(sem("sd_ready"), sum(1 for v in x_units if v <= u + 2))
                if i >= 1:
                    pe.wait_ge(sem("glo_ready"), i)
                for h in range(HEADS):
                    mm = pe.transpose(ps[:, h // 4, P * (h % 4):P * (h % 4) + P], tmp[:, i % 2, P * h:P * h + P], ident[:])
                mm.then_inc(sem("turned"), 1)

            front(0)
            for u in range(len(units)):
                if u + 1 < len(units):
                    front(u + 1)
                back(u)
                if u >= 1:
                    turn(u - 1)
            turn(len(units) - 1)

            pe.wait_ge(sem("glo_ready"), 8)
            for t in range(3):
                K = K_MOUT + t
                s = K % 2
                ks = range(3 * t, min(3 * t + 3, KT))
                pe.wait_ge(sem("lo_in"), K + 1 + CREDIT)
                pe.wait_ge(sem("lo_out"), K + 1 + CREDIT)
                for d in range(KT):
                    pe.wait_ge(sem("y_added"), 8 * (2 * FT + t) + d + 7)
                    for c in range(2):
                        for k in ks:
                            ws = slice(1024 * (k - 3 * t) + P * d, 1024 * (k - 3 * t) + P * d + P)
                            gh, gl = g_hi[:, 4 * c:4 * c + 4, k, :], g_lo[:, 4 * c:4 * c + 4, k, :]
                            mm = triple(ps[:, 4 + 2 * (d % 2) + c, :], w_hi[:, s, ws], w_lo[:, s, ws], gh, gl,
                                        k == ks[0], k == ks[-1])
                    mm.then_inc(sem("mo_part"), 1)
            norm("x_mlstm", TX)
            norm("x_pre2b", TX)
            ffn(p2, hx_hi, hx_lo, 8 * splits["x_pre2b"])
            norm("x_out", TX)

        @block.scalar
        def _(act):
            own = [0]

            def chain(ins):
                own[0] += 1
                ins.then_inc(sem("act_own"), 1)

            def own_done():
                act.wait_ge(sem("act_own"), own[0])

            def norm(key, T, src, ready):
                N = norms[key]
                for k in range(KT):
                    ready(k)
                    act.wait_ge(sem("sq_used"), 8 * N + k + 1)
                    act.activation(sq[:, k % 2, 0:T], src(k), ACT.Square).then_inc(sem("sq_ready"), 1)
                act.wait_ge(sem("sq_used"), 8 * N + 8 + CREDIT)
                act.activation(halves(rstd[N % 2][:, 0:T], T), ssq(T), ACT.Sqrt, bias=prmc(PM_EPS), scale=1.0 / D)\
                    .then_inc(sem("std_ready"), 1)

            def mod_round(r):
                act.wait_ge(sem("modw_used"), KT * (r + 1))
                if r >= 1:
                    act.wait_ge(sem("modcol_ready"), r)
                act.activation(modrow[:], ps[:, 0, :], ACT.Copy).then_inc(sem("modrow_ready"), 1)
                act.wait_ge(sem("modcol_ready"), r + 1)
                view = ps[:, 2, :].rearrange("p (b g x) -> p g b x", b=4, g=4)
                for s in range(2):
                    ins = act.activation(modt[:, s, 16 * r:16 * r + 16].rearrange("p (g b) -> p g b", b=4),
                                         view[:, :, :, s], ACT.Copy)
                ins.then_inc(sem("mod_done"), 1)

            def mixer(s, first):
                T = TOK[s]
                src, dst = (mix_in_x, mix_out_x) if s == "x" else (mix_in_c, mix_out_c)
                act.wait_ge(sem("derived"), 1)
                for k in range(KT):
                    act.wait_ge(sem("pooled"), first + k + 1)
                    act.activation(src[:, k, :], src[:, k, :], ACT.Copy, scale=derived(0, 0, s, k)).then_inc(sem("mix_in_ready"), 1)
                for d in range(KT):
                    act.wait_ge(sem("mix_done"), first + d + 1)
                    act.activation(dst[:, d, :], bank(4 + 2 * (d % 2), T), ACT.Copy, scale=prmc(PM_PS + d))\
                        .then_inc(sem("mix_out_ready"), 1)

            def norm_mix(s, first):
                dst = mix_out_x if s == "x" else mix_out_c
                norm(f"{s}_mix", TOK[s], lambda k: dst[:, k, :], lambda k: act.wait_ge(sem("mix_out_ready"), first + k + 1))

            def norm_pre(key, s, src, post, dst=None, counter=None):
                def ready(k):
                    act.wait_ge(sem("post_done"), 8 * post + k + 1)
                    if dst is not None:
                        act.dma_start(dst[:, k, :], src[:, k, :]).then_inc(sem(counter), 16)
                norm(key, TOK[s], lambda k: src[:, k, :], ready)

            def pre_hi(key, s, layer, which, src, dst):
                n = pres[key]
                for k in range(KT):
                    act.wait_ge(sem("pre_t"), 8 * n + k + 1)
                    act.activation(dst[:, k, :], src[:, k, :], ACT.Identity, bias=shift(layer, which, s, k))\
                        .then_inc(sem("pre_hi"), 1)

            def hi_in(turn, used, slot):
                act.wait_ge(sem(f"raw_in{slot}"), turn)
                act.wait_ge(sem("w_in_used"), used)
                act.activation(w_hi[:, slot, 0:2048], raw[:, slot, 0:2048], ACT.Copy).then_inc(sem("hi_done"), 1)

            def hi_out(used, slot):
                act.wait_ge(sem("w_out_used"), used)
                act.activation(w_hi[:, slot, 2048:WT], raw[:, slot, 2048:WT], ACT.Copy).then_inc(sem("hi_done"), 1)

            def hi_tile(K):
                slot = K % 2
                act.wait_ge(sem(f"raw_in{slot}"), 16 * (K // 2 + 1))
                for name, count in in_use(K - 2):
                    act.wait_ge(sem(name), count)
                act.activation(w_hi[:, slot, 0:2048], raw[:, slot, 0:2048], ACT.Copy).then_inc(sem("hi_done"), 1)
                act.activation(w_hi[:, slot, 2048:WT], raw[:, slot, 2048:WT], ACT.Copy).then_inc(sem("hi_done"), 1)

            def ffn(p):
                def tile(j, par, last=False):
                    act.wait_ge(sem("g_done"), j + (p.j0 + 1))
                    if not (isinstance(j, int) and j + p.j0 == 0):
                        act.wait_ge(sem("a_done"), j + p.j0)
                    cv = fcv[:, j + p.layer * FT, :] if not isinstance(j, int) else fcv[:, p.layer * FT + j, :]
                    act.activation(acc[:, 0:p.T], bank(0, p.T), ACT.Identity, bias=cv[:, 9:10], scale=cv[:, 4:5])\
                        .then_inc(sem("acc_ready"), 1)
                    s = (p.k0 + par + 1) % 2
                    if not last:
                        c = (p.k0 + par + 1) // 2 + 1
                        turn = (j - par) * 8 + 16 * c if not isinstance(j, int) else 16 * ((p.k0 + j + 1) // 2 + 1)
                        hi_in(turn, j + (p.j0 + 2), s)
                    act.wait_ge(sem("tap_done"), j * len(p.taps) + (p.tap0 + len(p.taps)))
                    act.activation(acc[:, 0:p.T], acc[:, 0:p.T], ACT.Silu).then_inc(sem("silu_done"), 1)
                    act.wait_ge(sem("a_done"), j + (p.j0 + 1))
                    act.wait_ge(sem("w_out_used"), j + (p.j0 + 1))
                    act.activation(a_hi[:, par, 0:p.T], prod[:, 0:p.T], ACT.Copy).then_inc(sem("a_hi_ready"), 1)
                    if not last:
                        hi_out(j + (p.j0 + 2), s)

                tile(0, 0)
                with act.Fori(0, FT // 2 - 1) as i:
                    tile(i * 2 + 1, 1)
                    tile(i * 2 + 2, 0)
                tile(FT - 1, 1, True)

            p0, p1, p2 = PASSES
            act.wait_ge(sem("const_in"), 7 * 16)
            act.wait_ge(sem("cpad_zero"), 1)
            act.activation(c_pad[:, :, 0:2], c_in[:], ACT.Silu).then_inc(sem("cpad_ready"), 1)
            norm("c_in", TC, lambda k: in_c[:, k, :], lambda k: act.wait_ge(sem("ctx_in"), 16))
            norm("x_in", TX, lambda k: y_x[:, k, :], lambda k: act.wait_ge(sem("x_in"), 16))
            for r in range(3):
                mod_round(r)
            mixer("c", 0)
            norm_mix("c", 0)
            norm_pre("c_pre2", "c", in_c, posts["c_mix"], xc_scr, "xc_out")
            for k in range(KT):
                act.wait_ge(sem("pre_t"), k + 1)
                act.activation(mix_in_c[:, k, :], in_c[:, k, :], ACT.Identity, bias=shift(0, 1, "c", k)).then_inc(sem("pre_hi"), 1)
            act.wait_ge(sem("pre_hi"), 8)
            act.dma_start(hc_scr, mix_in_c[:]).then_inc(sem("hc_out"), 16)
            mod_round(3)
            mixer("x", KT)
            norm_mix("x", KT)
            mod_round(4)
            norm_pre("x_pre2", "x", y_x, posts["x_mix"], x_scr[0], "x_out")
            mod_round(5)
            pre_hi("x_pre2", "x", 0, 1, y_x, hx_hi)
            act.wait_ge(sem("hc_out"), 16)
            hi_tile(p0.k0)
            ffn(p0)
            hi_tile(p1.k0)
            norm("x_ffn0", TX, lambda k: y_x[:, k, :], lambda k: act.wait_ge(sem("y_added"), 8 * (p0.y0 + FT) + k + 1))
            act.wait_ge(sem("hc_in"), 16)
            act.wait_ge(sem("w_in_used"), FT + CREDIT)
            for k in range(KT):
                act.activation(hc_hi[:, k, :], res_c[:, k, :], ACT.Copy).then_inc(sem("hc_hi"), 1)
            ffn(p1)
            hi_tile(K_MIN)
            norm("c_ffn", TC, lambda k: y_c[:, k, :], lambda k: act.wait_ge(sem("y_added"), 8 * (p1.y0 + FT) + k + 1))
            norm_pre("c_pre1", "c", y_c, posts["c_ffn"])
            pre_hi("c_pre1", "c", 1, 0, y_c, mc_hi)
            norm_pre("x_pre1", "x", y_x, posts["x_ffn0"], x_scr[1], "x_out")
            pre_hi("x_pre1", "x", 1, 0, y_x, hx_hi)

            e = 0
            for t in range(8):
                hi_tile(K_MIN + t + 1)
                for m in range(3 * t, min(3 * t + 3, 8)):
                    cv = prm[:, PM_MCV + 10 * m:PM_MCV + 10 * m + 10]
                    dst = q_x[:, m, :] if m < 4 else k_x[:, m - 4, :]
                    act.wait_ge(sem("qk_done"), m + 1)
                    if m >= 1:
                        own_done()
                    act.activation(acc[:], bank(2 * (m % 2), TX), ACT.Identity, bias=cv[:, 9:10], scale=cv[:, 4:5])\
                        .then_inc(sem("qacc_ready"), 1)
                    if m >= 4:
                        act.wait_ge(sem("kc_done"), m - 3)
                        act.activation(acc_c[:], ps[:, 4, 0:TC], ACT.Identity, bias=cv[:, 9:10], scale=cv[:, 4:5])\
                            .then_inc(sem("kcacc_ready"), 1)
                    act.wait_ge(sem("qtap_done"), 8 * (m + 1))
                    if m == 0:
                        act.wait_ge(sem("pre_lo"), 8 * splits["x_pre1"] + 8)
                    chain(act.activation(dst, acc[:], ACT.Silu))
                    if m >= 4:
                        own_done()
                        chain(act.activation(dst, dst, ACT.Copy, scale=0.125))
                        act.wait_ge(sem("kctap_done"), 2 * (m - 3))
                        chain(act.activation(k_c[:, m - 4, :], acc_c[:], ACT.Silu))
                        own_done()
                        chain(act.activation(k_c[:, m - 4, :], k_c[:, m - 4, :], ACT.Copy, scale=0.125))
                        own_done()
                while e < len(evacs) and evacs[e][0] == t:
                    _, n, m0, w = evacs[e]
                    act.wait_ge(sem("vo_done"), e + 1)
                    if e >= 2:
                        act.wait_ge(sem(f"stage_out{e % 2}"), stage_total[e - 2])
                    nv = max(0, min(16 - m0, w // P)) * P
                    out = ps[:, 5 + e % 3, 0:w]
                    if nv:
                        ins = act.activation(stage[:, e % 2, 0:nv], out[:, 0:nv], ACT.Copy)
                    if w > nv:
                        ins = act.activation(stage[:, e % 2, nv:w], out[:, nv:w], ACT.Sigmoid)
                    ins.then_inc(sem("stage_ready"), 1)
                    act.wait_ge(sem("stage_ready"), e + 1)
                    if nv:
                        act.dma_start(v_scr[n, :, P * (m0 - 8):P * (m0 - 8) + nv], stage[:, e % 2, 0:nv])\
                            .then_inc(sem(f"stage_out{e % 2}"), 16)
                    if w > nv:
                        c0 = P * (max(m0, 16) - 16)
                        act.dma_start(o_scr[n - 2, :, c0:c0 + w - nv], stage[:, e % 2, nv:w])\
                            .then_inc(sem(f"stage_out{e % 2}"), 16)
                    e += 1
            act.wait_ge(sem("gates_done"), 1)
            chain(act.activation(gates[:, TC:TC + TX], bank(0, TX), ACT.Identity, bias=prmc(PM_GB)))
            chain(act.activation(gates[:, 0:TC], ps[:, 2, 0:TC], ACT.Identity, bias=prmc(PM_GB)))
            own_done()
            f = slice(64, P)
            chain(act.activation(gtmp[f, :], gates[f, :], ACT.Abs))
            own_done()
            chain(act.activation(gtmp[f, :], gtmp[f, :], ACT.Exp, scale=-1.0))
            own_done()
            act.activation(gtmp[f, :], gtmp[f, :], ACT.Ln, bias=1.0).then_inc(sem("softplus"), 1)
            r64 = slice(0, 64)
            act.wait_ge(sem("gexp_in"), 1)
            act.activation(gw[r64, :], gw[r64, :], ACT.Exp).then_inc(sem("gates_ready"), 1)
            act.activation(gem[r64, :], gmax[r64, :], ACT.Exp, scale=-1.0).then_inc(sem("gates_ready"), 1)
            act.activation(ga[r64, :], ga[r64, :], ACT.Exp).then_inc(sem("rows_ready"), 1)
            act.activation(gend[r64, 3, :], gend[r64, 3, :], ACT.Exp).then_inc(sem("rows_ready"), 1)
            act.wait_ge(sem("gcols_done"), 1)
            flat = cols[:].rearrange("p n i r -> p (n i r)")
            for b in range(4):
                w = min(512, 64 * 3 * NCH - 512 * b)
                act.activation(flat[:, 512 * b:512 * b + w], ps[:, 4 + b, 0:w], ACT.Copy).then_inc(sem("cols_ready"), 1)

            def turned(u):
                if u in sec_index:
                    i, c = sec_index[u], units[u][1] - 2
                    act.wait_ge(sem("turned"), i + 1)
                    act.activation(g_hi[:, c, :, :].rearrange("p h t -> p (h t)"), bank(0, 1024), ACT.Copy).then_inc(sem("ghi_ready"), 1)

            def decay(u):
                if u in x_index:
                    act.wait_ge(sem("dexp_ready"), x_index[u] + 1)
                    act.activation(dmat[:, u % 2], dmat[:, u % 2], ACT.Exp).then_inc(sem("d_ready"), 1)

            decay(0)
            for u in range(len(units)):
                if u + 1 < len(units):
                    decay(u + 1)
                if u >= 1:
                    turned(u - 1)
            turned(len(units) - 1)
            for t in range(3):
                hi_tile(K_MOUT + t)
            hi_tile(p2.k0)
            norm("x_mlstm", TX, lambda k: y_x[:, k, :], lambda k: act.wait_ge(sem("y_added"), 8 * (2 * FT + 3) + k + 1))
            norm_pre("x_pre2b", "x", y_x, posts["x_mlstm"], x_scr[0], "x_out")
            pre_hi("x_pre2b", "x", 1, 1, y_x, hx_hi)
            ffn(p2)
            norm("x_out", TX, lambda k: y_x[:, k, :], lambda k: act.wait_ge(sem("y_added"), 8 * (p2.y0 + FT) + k + 1))

        @block.vector
        def _(dve):
            own = [0]

            def chain(ins):
                own[0] += 1
                ins.then_inc(sem("dve_own"), 1)

            def own_done():
                dve.wait_ge(sem("dve_own"), own[0])

            def norm(key, T):
                N = norms[key]
                dve.wait_ge(sem("std_ready"), N + 1)
                chain(dve.reciprocal(rstd[N % 2][:, 0:T], rstd[N % 2][:, 0:T]))
                own_done()
                return rstd[N % 2][:, 0:T]

            def pool(s, src, dst):
                T = TOK[s]
                R, W = GRID[s]
                Wp = W + 2 * PAD
                r = norm(f"{s}_in", T)
                z = zpad[:, 0:R * Wp].rearrange("p (r w) -> p r w", w=Wp)
                bufs = [b[:, 0:R * Wp].rearrange("p (r w) -> p r w", w=Wp) for b in (sum_a, sum_b)]
                inv = inv_x if s == "x" else inv_c
                chain(dve.memset(zpad[:], 0.0))
                for k in range(KT):
                    own_done()
                    chain(dve.tensor_tensor(z[:, :, PAD:PAD + W], grid(src[:, k, :], s), grid(r, s), ALU.mult))
                    own_done()
                    levels = k // 2 + 1
                    reach = [sum(2 ** (i - 1) for i in range(lv + 1, levels) if i >= 1) for lv in range(levels)]
                    cur = z
                    for lv in range(levels):
                        lo, hi = PAD - reach[lv], PAD + W + reach[lv]
                        back, fwd = (1, 0) if lv == 0 else (2 ** (lv - 1), 2 ** (lv - 1))
                        out = bufs[lv % 2]
                        chain(dve.tensor_tensor(out[:, :, lo:hi], cur[:, :, lo - back:hi - back],
                                                cur[:, :, lo + fwd:hi + fwd], ALU.add))
                        own_done()
                        cur = out
                    other = bufs[levels % 2]
                    weights = inv[:, k // 2, :].unsqueeze(1).broadcast_to([P, R, W])
                    chain(dve.tensor_tensor(other[:, :, PAD:PAD + W], cur[:, :, PAD:PAD + W], weights, ALU.mult))
                    own_done()
                    dve.tensor_tensor(grid(dst[:, k, :], s), other[:, :, PAD:PAD + W], z[:, :, PAD:PAD + W], ALU.subtract)\
                        .then_inc(sem("pooled"), 1)
                    dve.wait_ge(sem("pooled"), (0 if s == "c" else KT) + k + 1)

            def derive(layer):
                dve.wait_ge(sem("mod_done"), 3 * (layer + 1))
                lc = slice(48 * layer, 48 * layer + 48)
                for s in range(2):
                    chain(dve.tensor_tensor(modt[:, s, lc], modt[:, s, lc], prm[:, PM_MODB + 48 * layer:PM_MODB + 48 * layer + 48], ALU.add))
                own_done()
                for s in ("x", "c"):
                    for i, sec in enumerate((1, 2, 4, 5)):
                        g = prm[:, PM_G + 32 * layer + 8 * i:PM_G + 32 * layer + 8 * i + 8]
                        out = der[:, layer, 0 if s == "x" else 1, i, :]
                        if i % 2 == 0:
                            ins = dve.scalar_tensor_tensor(out, mod(layer, sec, s), 1.0, g, ALU.add, ALU.mult)
                        else:
                            ins = dve.tensor_tensor(out, mod(layer, sec, s), g, ALU.mult)
                ins.then_inc(sem("derived"), 1)
                dve.wait_ge(sem("derived"), layer + 1)

            def post(key, s, layer, which, y, x, out, ready=None):
                r = norm(key, TOK[s])
                for d in range(KT):
                    chain(dve.scalar_tensor_tensor(y[:, d, :], y[:, d, :], derived(layer, which, s, d), r, ALU.mult, ALU.mult))
                if ready is not None:
                    ready()
                for d in range(KT):
                    dve.wait_ge(sem("dve_own"), own[0] - KT + 1 + d)
                    dve.tensor_tensor(out[:, d, :], y[:, d, :], x[:, d, :], ALU.add).then_inc(sem("post_done"), 1)

            def pre_t(key, s, layer, which, src, stored=None):
                r = norm(key, TOK[s])
                if stored is not None:
                    dve.wait_ge(sem(stored[0]), stored[1])
                for d in range(KT):
                    dve.scalar_tensor_tensor(src[:, d, :], src[:, d, :], derived(layer, which, s, d), r, ALU.mult, ALU.mult)\
                        .then_inc(sem("pre_t"), 1)

            def pre_lo(key, s, layer, which, src, hi, lo):
                n = pres[key]
                for d in range(KT):
                    dve.wait_ge(sem("pre_hi"), 8 * n + d + 1)
                    dve.scalar_tensor_tensor(lo[:, d, :], src[:, d, :], shift(layer, which, s, d), hi[:, d, :].bitcast(F32),
                                             ALU.add, ALU.subtract).then_inc(sem("pre_lo"), 1)

            def lo_out(count, slot):
                dve.wait_ge(sem("hi_done"), count)
                dve.tensor_tensor(w_lo[:, slot, 2048:WT], raw[:, slot, 2048:WT], w_hi[:, slot, 2048:WT].bitcast(F32), ALU.subtract)\
                    .then_inc(sem("lo_out"), 1)

            def lo_tile(K):
                lo_out(2 * K + 2, K % 2)

            def ffn(p, y):
                NTAP = len(p.taps)

                def conv(j, par):
                    s = (p.k0 + par) % 2
                    lo_out(j * 2 + (2 * p.k0 + 2), s)
                    cv = fcv[:, j + p.layer * FT, :]
                    g, ac = grid(bank(0, p.T), p.stream), grid(acc[:, 0:p.T], p.stream)
                    dve.wait_ge(sem("acc_ready"), j + (p.j0 + 1))
                    for i, (r, c) in enumerate(p.taps):
                        out, src = tap_views(ac, g, r, c, p.R, p.W)
                        if i:
                            dve.wait_ge(sem("tap_done"), j * NTAP + (p.tap0 + i))
                        t = tap_index(r, c)
                        dve.scalar_tensor_tensor(out, src, cv[:, t:t + 1], out, ALU.mult, ALU.add).then_inc(sem("tap_done"), 1)

                def gate(j):
                    dve.wait_ge(sem("silu_done"), j + (p.j0 + 1))
                    dve.wait_ge(sem("w_in_used"), j + (p.j0 + 1 + CREDIT))
                    if not (isinstance(j, int) and j + p.j0 == 0):
                        dve.wait_ge(sem("a_lo_ready"), j + p.j0)
                    dve.tensor_tensor(prod[:, 0:p.T], acc[:, 0:p.T], bank(2, p.T), ALU.mult).then_inc(sem("a_done"), 1)

                def add(j, par):
                    for d in range(KT):
                        if d < 7:
                            dve.wait_ge(sem("y_part"), j * 7 + (7 * p.j0 + d + 1))
                        else:
                            dve.wait_ge(sem("w_out_used"), j + (p.j0 + 1 + CREDIT))
                        dve.wait_ge(sem("y_added"), j * 8 + (8 * p.y0 + d + 1))
                        dve.tensor_tensor(y[:, d, :], y[:, d, :], bank(4 + 2 * (d % 2), p.T), ALU.add).then_inc(sem("y_added"), 1)

                conv(0, 0)
                gate(0)
                dve.wait_ge(sem("y_zero"), p.index + 1)
                with dve.Fori(0, FT // 2 - 1) as i:
                    conv(i * 2 + 1, 1)
                    add(i * 2, 0)
                    gate(i * 2 + 1)
                    conv(i * 2 + 2, 0)
                    add(i * 2 + 1, 1)
                    gate(i * 2 + 2)
                conv(FT - 1, 1)
                add(FT - 2, 0)
                gate(FT - 1)
                add(FT - 1, 1)

            p0, p1, p2 = PASSES
            for name, n in (("sq_used", 2), ("w_in_used", 2), ("w_out_used", 2), ("lo_in", 2), ("lo_out", 2), ("y_added", 8)):
                dve.sem_inc(sem(name), n)
            dve.memset(ones[:], 1.0).then_inc(sem("ones_ready"), 1)
            dve.memset(c_pad[:], 0.0).then_inc(sem("cpad_zero"), 1)
            dve.wait_ge(sem("const_in"), 7 * 16)
            pool("c", in_c, mix_in_c)
            pool("x", y_x, mix_in_x)
            derive(0)
            post("c_mix", "c", 0, 1, mix_out_c, in_c, in_c)
            pre_t("c_pre2", "c", 0, 2, in_c, ("xc_out", 16 * KT))
            post("x_mix", "x", 0, 1, mix_out_x, y_x, y_x)
            pre_t("x_pre2", "x", 0, 2, y_x, ("x_out", 16 * KT))
            pre_lo("x_pre2", "x", 0, 1, y_x, hx_hi, hx_lo)
            ffn(p0, y_x)
            post("x_ffn0", "x", 0, 3, y_x, res_x, y_x, lambda: dve.wait_ge(sem("res_in"), 16))
            derive(1)
            ffn(p1, y_c)
            post("c_ffn", "c", 0, 3, y_c, res_c, y_c, lambda: dve.wait_ge(sem("resc_in"), 16))
            pre_t("c_pre1", "c", 1, 0, y_c)
            pre_lo("c_pre1", "c", 1, 0, y_c, mc_hi, mc_lo)
            pre_t("x_pre1", "x", 1, 0, y_x, ("x_out", 32 * KT))
            dve.wait_ge(sem("pre_lo"), 8 * splits["c_pre1"] + 8)
            pre_lo("x_pre1", "x", 1, 0, y_x, hx_hi, hx_lo)
            lo_tile(K_MIN)

            for t in range(8):
                lo_tile(K_MIN + t + 1)
                for m in range(3 * t, min(3 * t + 3, 8)):
                    cv = prm[:, PM_MCV + 10 * m:PM_MCV + 10 * m + 10]
                    dve.wait_ge(sem("qacc_ready"), m + 1)
                    for i, (r, c) in enumerate(taps_of("x")):
                        out, src = tap_views(grid(acc[:], "x"), grid(bank(2 * (m % 2), TX), "x"), r, c, *GRID["x"])
                        if i:
                            dve.wait_ge(sem("qtap_done"), 8 * m + i)
                        tt = tap_index(r, c)
                        dve.scalar_tensor_tensor(out, src, cv[:, tt:tt + 1], out, ALU.mult, ALU.add).then_inc(sem("qtap_done"), 1)
                    if m >= 4:
                        dve.wait_ge(sem("kcacc_ready"), m - 3)
                        for i, (r, c) in enumerate(taps_of("c")):
                            out, src = tap_views(grid(acc_c[:], "c"), grid(ps[:, 4, 0:TC], "c"), r, c, *GRID["c"])
                            if i:
                                dve.wait_ge(sem("kctap_done"), 2 * (m - 4) + i)
                            tt = tap_index(r, c)
                            dve.scalar_tensor_tensor(out, src, cv[:, tt:tt + 1], out, ALU.mult, ALU.add).then_inc(sem("kctap_done"), 1)

            f64 = slice(64, P)
            r64 = slice(0, 64)
            fw, bw = slice(0, 8), slice(32, 40)
            dve.wait_ge(sem("gates_done"), 1)
            dve.wait_ge(sem("lo_out"), K_GATE + 1 + CREDIT)
            for t_ in (gcum, gmax):
                chain(dve.memset(t_[r64, :], 0.0))
            chain(dve.memset(greset[r64, :], 1.0))
            chain(dve.memset(gend[r64], 0.0))
            own_done()
            r3 = greset[:].rearrange("p (n t) -> p n t", t=CH)
            chain(dve.memset(r3[0:32, :, 0:1], 0.0))
            chain(dve.memset(r3[32:64, :, CH - 1:CH], 0.0))
            dve.wait_ge(sem("softplus"), 1)
            chain(dve.scalar_tensor_tensor(logf[r64, :], gates[f64, :], 0.0, gtmp[f64, :], ALU.min, ALU.subtract))
            own_done()
            chain(dve.tensor_tensor_scan(gcum[fw, :], greset[fw, :], logf[fw, :], 0.0, ALU.mult, ALU.add))
            chain(dve.tensor_tensor_scan(gcum[bw, :][:, ::-1], greset[bw, :][:, ::-1], logf[bw, :][:, ::-1], 0.0, ALU.mult, ALU.add))
            chain(dve.tensor_tensor_scan(gmax[fw, :], logf[fw, :], gates[fw, :], 0.0, ALU.add, ALU.max))
            chain(dve.tensor_tensor_scan(gmax[bw, 0:TC][:, ::-1], logf[bw, 0:TC][:, ::-1], gates[bw, 0:TC][:, ::-1], 0.0,
                                         ALU.add, ALU.max))
            own_done()
            chain(dve.tensor_tensor_scan(gmax[bw, TC:NT][:, ::-1], logf[bw, TC:NT][:, ::-1], gates[bw, TC:NT][:, ::-1],
                                         gmax[bw, 0:1], ALU.add, ALU.max))
            own_done()
            b3 = gcum[:].rearrange("p (n t) -> p n t", t=CH)
            m3 = gmax[:].rearrange("p (n t) -> p n t", t=CH)
            f, b = slice(0, 32), slice(32, 64)
            chain(dve.tensor_copy(gend[f, 0, 1:NCH], m3[f, 0:NCH - 1, CH - 1]))
            chain(dve.tensor_copy(gend[b, 0, 2:NCH - 1], m3[b, 3:NCH, 0]))
            chain(dve.tensor_copy(gend[b, 0, NCH - 1:NCH], m3[b, 0, 0:1]))
            chain(dve.tensor_copy(gend[b, 0, 0:1], m3[b, 1, 0:1]))
            chain(dve.tensor_tensor(gend[f, 1, :], b3[f, :, CH - 1], m3[f, :, CH - 1], ALU.subtract))
            chain(dve.tensor_tensor(gend[b, 1, :], b3[b, :, 0], m3[b, :, 0], ALU.subtract))
            chain(dve.tensor_tensor(gc_[r64, :], gates[r64, :], gcum[r64, :], ALU.subtract))
            dve.tensor_tensor(gr[r64, :], gcum[r64, :], gmax[r64, :], ALU.subtract).then_inc(sem("rows_ready"), 1)
            own_done()
            dve.wait_ge(sem("rows_ready"), 1)

            def spread(i):
                return gend[r64, i, :].unsqueeze(2).broadcast_to([64, NCH, CH])

            def chunks(t_):
                return t_[r64, :].rearrange("p (n t) -> p n t", t=CH)

            chain(dve.tensor_tensor(gend[r64, 3, :], gend[r64, 0, :], gend[r64, 1, :], ALU.add))
            chain(dve.tensor_tensor(chunks(ga), chunks(gr), spread(0), ALU.add))
            dve.tensor_tensor(chunks(gw), chunks(gc_), spread(1), ALU.add).then_inc(sem("gexp_in"), 1)
            own_done()
            dve.wait_ge(sem("cols_ready"), 4)
            dve.wait_ge(sem("rows_out"), 48)
            dve.memset(state[:], 0.0).then_inc(sem("state_zero"), 1)
            dve.memset(vch[:, :, :, P:P + 1], 1.0).then_inc(sem("state_zero"), 1)
            dve.wait_ge(sem("state_zero"), 2)
            dve.wait_ge(sem("alpha_in"), 64)

            def col(n, i, dr):
                return cols[:, n, i, 32 * dr:32 * dr + 8]

            def front(u):
                dr, n = units[u]
                dve.wait_ge(sem("kt_done"), u + 1)
                if u >= 2:
                    dve.wait_ge(sem("unit_done"), u - 1)
                dve.tensor_tensor(kw[:, u % 2, :].rearrange("p (h k) -> p h k", k=64), ps[:, 5, :].rearrange("p (h k) -> p h k", k=64),
                                  col(n, 1, dr).unsqueeze(2).broadcast_to([P, HEADS, 64]), ALU.mult).then_inc(sem("kw_ready"), 1)
                if n >= 2:
                    i = x_index[u]
                    dve.wait_ge(sem("masked"), i + 1)
                    dm = dmat[:, u % 2].rearrange("p (a b) t -> p a b t", a=2)
                    cc = col(n, 0, dr).rearrange("p (b a) -> p a b", a=2)
                    for par in range(2):
                        ins = dve.tensor_tensor(dm[:, par], dm[:, par], cc[:, par, :].unsqueeze(2).broadcast_to([P, 4, CH]), ALU.add)
                    ins.then_inc(sem("dexp_ready"), 1)
                    dve.wait_ge(sem("d_ready"), i + 1)
                    dve.wait_ge(sem("s_done"), i + 1)
                    dve.tensor_tensor(dmat[:, u % 2].rearrange("p h t -> p (h t)"), dmat[:, u % 2].rearrange("p h t -> p (h t)"),
                                      bank(0, 1024), ALU.mult).then_inc(sem("sd_ready"), 1)

            def back(u):
                dr, n = units[u]
                if n >= 2:
                    i = x_index[u]
                    dve.wait_ge(sem("num_done"), i + 1)
                    if i >= 1:
                        dve.wait_ge(sem("hs_ready"), i)
                    num = ps[:, 2:4, 0:387].rearrange("p b (j v) -> p b j v", v=P + 1)
                    num2 = ps[:, 4, 0:258].rearrange("p (j v) -> p j v", v=P + 1)
                    chain(dve.tensor_copy(dens[:, 0, 0:6].rearrange("p (b j) -> p b j", j=3), num[:, :, :, P]))
                    chain(dve.tensor_copy(dens[:, 0, 6:8], num2[:, :, P]))
                    own_done()
                    chain(dve.scalar_tensor_tensor(dens[:, 1, :], dens[:, 0, :], -1.0, dens[:, 0, :], ALU.mult, ALU.max))
                    own_done()
                    chain(dve.tensor_tensor(dens[:, 1, :], dens[:, 1, :], col(n, 2, dr), ALU.max))
                    own_done()
                    chain(dve.reciprocal(dens[:, 2, :], dens[:, 1, :]))
                    own_done()
                    if u in sec_index:
                        si = sec_index[u]
                        if si >= 2:
                            dve.wait_ge(sem("turned"), si - 1)
                        dst = tmp[:, si % 2, :]
                    else:
                        dst = hs[:, n - 2, :]
                    dst = dst.rearrange("p (h v) -> p h v", v=P)
                    for b_ in range(2):
                        dve.tensor_tensor(dst[:, 3 * b_:3 * b_ + 3, :], num[:, b_, :, 0:P],
                                          dens[:, 2, 3 * b_:3 * b_ + 3].unsqueeze(2).broadcast_to([P, 3, P]), ALU.mult)
                    dve.tensor_tensor(dst[:, 6:8, :], num2[:, :, 0:P], dens[:, 2, 6:8].unsqueeze(2).broadcast_to([P, 2, P]), ALU.mult)\
                        .then_inc(sem("hs_ready"), 1)
                dve.wait_ge(sem("unit_done"), u + 1)
                if u >= 2:
                    dve.wait_ge(sem("state_ready"), 8 * (u - 1))
                for h in range(HEADS):
                    pair, par = h // 2, h % 2
                    r = slice(64 * par, 64 * par + 64)
                    dve.scalar_tensor_tensor(state[r, dr, h, :], state[r, dr, h, :], alpha[r, dr, pair, n:n + 1],
                                             ps[r, 6 + pair // 3, (P + 1) * (pair % 3):(P + 1) * (pair % 3 + 1)], ALU.mult, ALU.add)\
                        .then_inc(sem("state_ready"), 1)

            def turned(u):
                if u in sec_index:
                    i, c = sec_index[u], units[u][1] - 2
                    dve.wait_ge(sem("ghi_ready"), i + 1)
                    dve.tensor_tensor(g_lo[:, c].rearrange("p h t -> p (h t)"), bank(0, 1024),
                                      g_hi[:, c].rearrange("p h t -> p (h t)").bitcast(F32), ALU.subtract).then_inc(sem("glo_ready"), 1)

            front(0)
            for u in range(len(units)):
                if u + 1 < len(units):
                    front(u + 1)
                back(u)
                if u >= 1:
                    turned(u - 1)
            turned(len(units) - 1)
            for t in range(3):
                lo_tile(K_MOUT + t)
                for d in range(KT):
                    dve.wait_ge(sem("mo_part"), 8 * t + d + 1)
                    dve.wait_ge(sem("y_added"), 8 * (2 * FT + t) + d + 1)
                    b_ = bank(4 + 2 * (d % 2), TX)
                    ins = dve.tensor_copy(y_x[:, d, :], b_) if t == 0 else dve.tensor_tensor(y_x[:, d, :], y_x[:, d, :], b_, ALU.add)
                    ins.then_inc(sem("y_added"), 1)
            post("x_mlstm", "x", 1, 1, y_x, res_x, y_x, lambda: dve.wait_ge(sem("res_in"), 32))
            pre_t("x_pre2b", "x", 1, 2, y_x, ("x_out", 48 * KT))
            pre_lo("x_pre2b", "x", 1, 1, y_x, hx_hi, hx_lo)
            ffn(p2, y_x)
            post("x_out", "x", 1, 3, y_x, res_x, y_x, lambda: dve.wait_ge(sem("res_in"), 48))

        @block.gpsimd
        def _(pool):
            def lo_in(count, slot):
                pool.wait_ge(sem("hi_done"), count)
                pool.tensor_tensor(w_lo[:, slot, 0:2048], raw[:, slot, 0:2048], w_hi[:, slot, 0:2048].bitcast(F32), ALU.subtract)\
                    .then_inc(sem("lo_in"), 1)

            def lo_tile(K):
                lo_in(2 * K + 1, K % 2)

            def ffn(p):
                def tile(j, par, last=False):
                    if not last:
                        lo_in(j * 2 + (2 * p.k0 + 3), (p.k0 + par + 1) % 2)
                    pool.wait_ge(sem("a_hi_ready"), j + (p.j0 + 1))
                    pool.tensor_tensor(a_lo[:, par, 0:p.T], prod[:, 0:p.T], a_hi[:, par, 0:p.T].bitcast(F32), ALU.subtract)\
                        .then_inc(sem("a_lo_ready"), 1)

                tile(0, 0)
                with pool.Fori(0, FT // 2 - 1) as i:
                    tile(i * 2 + 1, 1)
                    tile(i * 2 + 2, 0)
                tile(FT - 1, 1, True)

            def clear(p, y, free):
                free()
                pool.memset(y[:], 0.0).then_inc(sem("y_zero"), 1)

            p0, p1, p2 = PASSES
            lo_tile(p0.k0)
            clear(p0, y_x, lambda: pool.wait_ge(sem("pre_lo"), 8))
            ffn(p0)
            lo_tile(p1.k0)
            for k in range(KT):
                pool.wait_ge(sem("hc_hi"), k + 1)
                pool.tensor_tensor(hc_lo[:, k, :], res_c[:, k, :], hc_hi[:, k, :].bitcast(F32), ALU.subtract).then_inc(sem("hc_split"), 1)
            clear(p1, y_c, lambda: None)
            ffn(p1)
            for t in range(9):
                lo_tile(K_MIN + t)
            for u, (dr, n) in enumerate(units):
                if n >= 2:
                    i = x_index[u]
                    if i == 0:
                        pool.wait_ge(sem("mask_in"), 16)
                    pool.wait_ge(sem(f"row_in{u % 2}"), 64 * (i // 2 + 1))
                    pool.tensor_tensor(dmat[:, u % 2], dmat[:, u % 2], masks[:, dr, :].unsqueeze(1).broadcast_to([P, HEADS, CH]), ALU.add)\
                        .then_inc(sem("masked"), 1)
                    pool.tensor_tensor(qa[:, u % 2], qa[:, u % 2], q_x[:, :, (n - 2) * CH:(n - 1) * CH], ALU.mult)\
                        .then_inc(sem("qa_ready"), 1)
                for v in ([u - 1] if u < len(units) - 1 else [u - 1, u]):
                    if v in sec_index:
                        i = sec_index[v]
                        c = units[v][1] - 2
                        pool.wait_ge(sem("hs_ready"), x_index[v] + 1)
                        pool.tensor_tensor(tmp[:, i % 2, :], tmp[:, i % 2, :], hs[:, c, :], ALU.add).then_inc(sem("both"), 1)
                        pool.wait_ge(sem("both"), i + 1)
                        pool.wait_ge(sem("o_in"), 16 * (i + 1))
                        pool.tensor_tensor(tmp[:, i % 2, :], tmp[:, i % 2, :], och[:], ALU.mult).then_inc(sem("gated"), 1)
            for t in range(3):
                lo_tile(K_MOUT + t)
            lo_tile(p2.k0)
            clear(p2, y_x, lambda: pool.wait_ge(sem("pre_lo"), 8 * splits["x_pre2b"] + 8))
            ffn(p2)


_INS = ["x", "ctx", "ccol", "prm", "fcv", "ident", "inv_x", "inv_c", "pool_w", "modw", "ffn_w", "mlstm_w", "masks"]


def lay_out(x, c, ctx, c_ctx, mod_w, mod_b, norm_g, pool_w, pool_scale, mlstm_w_in, mlstm_b_gate,
            mlstm_conv_w, mlstm_conv_b, mlstm_w_out, ffn_w_in, ffn_conv_w, ffn_conv_b, ffn_w_out):
    f = np.float32

    def cols(v):
        return np.asarray(v).reshape(-1, P).T

    def act(v):
        return np.ascontiguousarray(np.asarray(v).T.reshape(KT, P, -1).transpose(1, 0, 2))

    def conv(w, b):
        both = np.concatenate([np.asarray(w).reshape(9, -1), np.asarray(b)[None]], 0)
        return both.reshape(10, -1, P).transpose(2, 1, 0)

    a = {"x": act(x[0]), "ctx": act(ctx[0])}
    a["ccol"] = np.ascontiguousarray(np.stack([cols(c[0]), cols(c_ctx)], -1))
    gate_cols = np.concatenate([np.arange(8) + 32 * i for i in range(4)])
    gb = np.zeros((P,), f)
    gb[gate_cols] = np.asarray(mlstm_b_gate)[0]
    a["prm"] = np.ascontiguousarray(np.concatenate(
        [cols(mod_b[0]), cols(mod_b[1]), cols(np.asarray(norm_g).reshape(-1)), cols(pool_scale[0]),
         conv(mlstm_conv_w[0], mlstm_conv_b[0]).reshape(P, -1), gb[:, None], np.full((P, 1), EPS, f)], 1))
    assert a["prm"].shape[1] == N_PRM
    a["fcv"] = np.ascontiguousarray(np.concatenate([conv(ffn_conv_w[l], ffn_conv_b[l]) for l in range(2)], 1))
    a["ident"] = np.eye(P, dtype=f)
    for name, W in (("inv_x", 64), ("inv_c", 256)):
        pos = np.arange(W)
        inv = [1.0 / (np.clip(pos - w // 2 + w, 0, W) - np.clip(pos - w // 2, 0, W)) for w in WINDOWS]
        a[name] = np.ascontiguousarray(np.broadcast_to(np.stack(inv).astype(f), (P, 4, W)))
    a["pool_w"] = np.ascontiguousarray(np.asarray(pool_w)[0].reshape(4, 2, P, 256).transpose(2, 0, 1, 3))
    a["modw"] = np.ascontiguousarray(
        np.asarray(mod_w).reshape(2, KT, P, 3, 2048).transpose(0, 3, 1, 2, 4).reshape(48, P, 2048))
    w_in = np.asarray(ffn_w_in).reshape(2, KT, P, 2, FT, P).transpose(0, 4, 2, 3, 1, 5)
    w_out = np.asarray(ffn_w_out).reshape(2, FT, P, D)
    a["ffn_w"] = np.concatenate([w_in[:, :, :, 1].reshape(2, FT, P, D), w_in[:, :, :, 0].reshape(2, FT, P, D), w_out], -1)\
        .reshape(2 * FT, P, WT)
    wm = np.asarray(mlstm_w_in)[0]
    tiles = list(wm[:, :WT].reshape(KT, P, 8, 384).transpose(2, 1, 0, 3).reshape(8, P, WT))
    gate = np.zeros((P, WT), f)
    gate[:, :1024].reshape(P, KT, P)[:, :, gate_cols] = wm[:, WT:].reshape(KT, P, 32).transpose(1, 0, 2)
    wo = np.zeros((9, P, D), f)
    wo[:8] = np.asarray(mlstm_w_out)[0].reshape(8, P, D)
    a["mlstm_w"] = np.ascontiguousarray(np.stack(tiles + [gate] + list(wo.reshape(3, 3, P, D).transpose(0, 2, 1, 3).reshape(3, P, WT))))
    s, t = np.arange(CH)[:, None], np.arange(CH)[None]
    a["masks"] = np.ascontiguousarray(np.stack([np.where(s <= t, 0.0, MASKED), np.where(s >= t, 0.0, MASKED)], 1).astype(f))
    return a


def kernel(**inputs):
    import concourse.bacc as _bacc
    from concourse.bass_utils import run_bass_kernel_spmd as _run

    arrays = lay_out(**inputs)
    nc = _bacc.Bacc("TRN2", target_bir_lowering=False, num_devices=1)
    args = {n: nc.dram_tensor(f"in_{n}", arrays[n].shape, F32, kind="ExternalInput").ap() for n in _INS}
    args["out"] = nc.dram_tensor("out_x", (P, KT, TX), F32, kind="ExternalOutput").ap()
    build(nc, args)
    r = _run(nc, [{f"in_{n}": arrays[n] for n in _INS}], core_ids=[0])
    out = r.results[0]["out_x"]
    return out.transpose(1, 0, 2).reshape(D, TX).T.reshape(1, TX, D)
```

```python
from contextlib import ExitStack

import numpy as np

import concourse.bass as bass
from concourse import mybir

F32 = mybir.dt.float32
F32R = mybir.dt.float32r
ALU = mybir.AluOpType
ACT = mybir.ActivationFunctionType

P = 128
D = 1024
KT = D // P
TX = 1024
TC = 256
GRID = {"x": (16, 64), "c": (1, 256)}
TOK = {"x": TX, "c": TC}
DFF = 2816
FT = DFF // P
HEADS = 8
CH = 128
NCH = (TX + TC) // CH
EPS = 1e-6
WINDOWS = (2, 4, 8, 16)
PAD = 8
WT = 3072
CREDIT = 2
MASKED = -1e30

MODC = 12

K_FFN0, K_FFNC, K_MIN, K_GATE, K_MOUT = 0, FT, 2 * FT, 2 * FT + 8, 2 * FT + 9
K_FFN1 = K_MOUT + 3
PM_MODB, PM_G, PM_PS, PM_MCV, PM_GB, PM_EPS = 0, 96, 160, 168, 248, 249
N_PRM = 250


class Pass:

    def __init__(self, index, stream, layer, k0, y0, tap0):
        self.index, self.stream, self.layer = index, stream, layer
        self.T = TOK[stream]
        self.R, self.W = GRID[stream]
        self.chunks = max(1, self.T // 512)
        self.cw = self.T // self.chunks
        self.j0 = index * FT
        self.k0 = k0
        self.y0 = y0
        self.tap0 = tap0
        self.parts0 = (0, 7 * FT, 10 * FT)[index]
        self.taps = taps_of(stream)


def taps_of(stream):
    rows = (-1, 0, 1) if GRID[stream][0] > 1 else (0,)
    return [(r, c) for r in rows for c in (-1, 0, 1) if (r, c) != (0, 0)]


def tap_index(r, c):
    return 3 * (r + 1) + c + 1


def tap_views(dst, src, r, c, R, W):
    r0, r1 = max(0, -r), min(R, R - r)
    c0, c1 = max(0, -c), min(W, W - c)
    return dst[:, r0:r1, c0:c1], src[:, r0 + r:r1 + r, c0 + c:c1 + c]


PASSES = [Pass(0, "x", 0, K_FFN0, 0, 0),
          Pass(1, "c", 0, K_FFNC, FT, 8 * FT),
          Pass(2, "x", 1, K_FFN1, 2 * FT + 3, 8 * FT + 2 * FT)]


def build(nc, a):
    with ExitStack() as ctx:
        sems = {}

        def sem(name):
            if name not in sems:
                sems[name] = ctx.enter_context(nc.semaphore(name))
            return sems[name]

        base = (nc.sbuf_base + 63) // 64 * 64

        def at(name, offset, shape, dt=F32):
            return nc.alloc_sbuf_tensor_at(name, shape, dt, offset=base + offset)

        H_HI, H_LO, Y_AT, RAW, W_HI, W_LO, WORK = 0, 32768, 65536, 98304, 122880, 147456, 172032
        SMALL = WORK + 32768

        hx_hi = at("hx_hi", H_HI, [P, KT, TX], F32R)
        hx_lo = at("hx_lo", H_LO, [P, KT, TX], F32R)
        y_x = at("y_x", Y_AT, [P, KT, TX])
        mix_in_x = at("mix_in_x", H_HI, [P, KT, TX])
        mix_out_x = at("mix_out_x", H_LO, [P, KT, TX])
        res_x = at("res_x", H_HI, [P, KT, TX])
        hc_hi = at("hc_hi", H_LO, [P, KT, TC], F32R)
        hc_lo = at("hc_lo", H_LO + 8192, [P, KT, TC], F32R)
        y_c = at("y_c", H_LO + 16384, [P, KT, TC])
        res_c = at("res_c", H_LO + 24576, [P, KT, TC])
        raw = at("raw", RAW, [P, 2, WT])
        w_hi = at("w_hi", W_HI, [P, 2, WT], F32R)
        w_lo = at("w_lo", W_LO, [P, 2, WT], F32R)
        modw = at("modw", RAW, [P, 4, 2048])
        in_c = at("in_c", W_HI + 8192, [P, KT, TC])
        mix_in_c = at("mix_in_c", W_HI + 16384, [P, KT, TC])
        mix_out_c = at("mix_out_c", W_LO, [P, KT, TC])
        pool_w = at("pool_w", W_LO + 8192, [P, 4, 2, 256])
        inv_x = at("inv_x", W_LO + 16384, [P, 4, 64])
        inv_c = at("inv_c", W_LO + 16384 + 1024, [P, 4, 256])
        modrow = at("modrow", W_LO + 21504, [P, 512])
        modw1 = at("modw1", H_HI, [P, KT, 512])
        modrow1 = at("modrow1", WORK + 28672, [P, 512])
        acc = at("acc", WORK, [P, TX])
        prod = at("prod", WORK + 4096, [P, TX])
        a_hi = at("a_hi", WORK + 8192, [P, 2, TX], F32R)
        a_lo = at("a_lo", WORK + 16384, [P, 2, TX], F32R)
        sq = at("sq", WORK, [P, 2, TX])
        zpad = at("zpad", WORK + 8192, [P, 1280])
        sum_a = at("sum_a", WORK + 13312, [P, 1280])
        sum_b = at("sum_b", WORK + 18432, [P, 1280])
        rstd = [at(f"rstd{i}", WORK + 24576 + 1024 * i, [P, TX // 4]) for i in range(3)]
        q_x = at("q_x", Y_AT, [P, 4, TX])
        k_x = at("k_x", Y_AT + 16384, [P, 4, TX])
        acc_c = at("acc_c", WORK + 4096, [P, TC])
        mc_hi = at("mc_hi", WORK + 8192, [P, KT, TC], F32R)
        mc_lo = at("mc_lo", WORK + 16384, [P, KT, TC], F32R)
        k_c = at("k_c", WORK + 24576, [P, 4, TC])
        stage = at("stage", WORK + 28672, [P, 2, 384])
        NT = NCH * CH
        gates = at("gates", WORK, [P, NT])
        gtmp = at("gtmp", WORK + 5120, [P, NT])
        logf = at("logf", WORK + 10240, [P, NT])
        gcum = at("gcum", WORK + 15360, [P, NT])
        GA = W_HI
        gmax = at("gmax", GA, [P, NT])
        gr = at("gr", GA + 5120, [P, NT])
        gc_ = at("gc", GA + 10240, [P, NT])
        gw = at("gw", GA + 15360, [P, NT])
        ga = at("ga", GA + 20480, [P, NT])
        gem = at("gem", GA + 25600, [P, NT])
        greset = at("greset", GA + 30720, [P, NT])
        cols = at("cols", GA + 41088, [P, NCH, 3, 64])
        alpha = at("alpha", GA + 48768, [P, 2, 4, NCH])
        gend = at("gend", WORK + 20480, [P, 4, NCH])
        dmat = at("dmat", GA, [P, 3, HEADS, CH])
        qa = at("qa", GA + 12288, [P, 3, 4, CH])
        vch = at("vch", GA + 18432, [P, 2, HEADS, P + 1])
        kw = at("kw", GA + 26688, [P, 2, 512])
        state = at("state", GA + 30784, [P, 2, HEADS, P + 1])
        och = at("och", WORK + 16384, [P, 2, 1024])
        tmp = at("tmp", WORK + 4096, [P, 2, 1024])
        masks = at("masks", WORK + 12288, [P, 2, CH])
        hs = at("hs", H_LO, [P, 8, 1024])
        g_hi = at("g_hi", H_HI, [P, 8, HEADS, CH], F32R)
        g_lo = at("g_lo", H_LO, [P, 8, HEADS, CH], F32R)
        small = [SMALL]

        def little(name, shape, dt=F32):
            t = at(name, small[0], shape, dt)
            small[0] += (4 * int(np.prod(shape[1:])) + 31) // 32 * 32
            return t

        prm = little("prm", [P, N_PRM])
        fcv = little("fcv", [P, 2 * FT, 10])
        modt = little("modt", [P, 2, 96])
        der = little("der", [P, 2, 2, 4, KT])
        c_in = little("c_in", [P, KT, 2])
        c_pad = little("c_pad", [P, KT, 32])
        ident = little("ident", [P, P])
        ones = little("ones", [P, 32])
        fold = little("fold", [P, 2])
        pick = little("pick", [P, 4, P])
        dens = little("dens", [P, 3, HEADS])
        assert base + small[0] <= nc.SBUF_PARTITION_SIZE_BYTES
        ps = ctx.enter_context(nc.psum_tensor("ps", [P, 8, 512], F32))

        def scratch(name, shape):
            return nc.dram_tensor(name, shape, F32, kind="Internal").ap()

        x_scr = scratch("x_scr", (2, P, KT, TX))
        xc_scr = scratch("xc_scr", (P, KT, TC))
        hc_scr = scratch("hc_scr", (P, KT, TC))
        v_scr = scratch("v_scr", (NCH, P, 1024))
        o_scr = scratch("o_scr", (8, P, 1024))
        row_scr = scratch("row_scr", (2, 64, NT))
        al_scr = scratch("al_scr", (64, NCH))

        def bank(b0, T):
            v = ps[:, b0:b0 + 2, :].rearrange("p b n -> p (b n)")
            return v[:, 0:T]

        def ssq(T):
            return ps[:, 1, 0:T // 4]

        def roots(T):
            return bank(6, T) if T == TX else ps[:, 3, 0:T]

        def grid(ap, s):
            return ap.rearrange("p (r w) -> p r w", w=GRID[s][1])

        def mod(layer, sec, s):
            c0 = layer * 48 + sec * 8
            return modt[:, 0 if s == "x" else 1, c0:c0 + 8]

        def derived(layer, which, s, d):
            return der[:, layer, 0 if s == "x" else 1, which, d:d + 1]

        def shift(layer, which, s, d):
            c0 = layer * 48 + 24 * which + d
            return modt[:, 0 if s == "x" else 1, c0:c0 + 1]

        def prmc(c):
            return prm[:, c:c + 1]

        norms = {k: n for n, k in enumerate(["c_in", "x_in", "c_mix", "c_pre2", "x_mix", "x_pre2", "x_ffn0", "x_pre1",
                                             "c_ffn", "c_pre1", "x_mlstm", "x_pre2b", "x_out"])}
        spreads = {k: n for n, k in enumerate(["c_in", "x_in", "c_mix", "c_pre2", "x_mix", "x_pre2", "x_ffn0",
                                               "c_ffn", "c_pre1", "x_pre1", "x_mlstm", "x_pre2b", "x_out"])}
        posts = {k: n for n, k in enumerate(["c_mix", "x_mix", "x_ffn0", "c_ffn", "x_mlstm", "x_out"])}
        pres = {k: n for n, k in enumerate(["c_pre2", "x_pre2", "c_pre1", "x_pre1", "x_pre2b"])}

        splits = {k: n for n, k in enumerate(["x_pre2", "c_pre1", "x_pre1", "x_pre2b"])}

        order_b = [1, 0] + list(range(NCH - 1, 1, -1))
        units = []
        for s in range(NCH):
            units += [(0, s), (1, order_b[s])]
        x_units = [u for u, (_, n) in enumerate(units) if n >= 2]
        x_index = {u: i for i, u in enumerate(x_units)}
        seen, second = set(), []
        for u in x_units:
            n = units[u][1]
            if n in seen:
                second.append(u)
            seen.add(n)
        sec_index = {u: i for i, u in enumerate(second)}
        evacs = []
        for t in range(8):
            m0 = max(3 * t, 8)
            w = (3 * t + 3 - m0) * P
            if w <= 0:
                continue
            for n in range(NCH):
                cw = w if n >= 2 else max(0, min(16, 3 * t + 3) - m0) * P
                if cw:
                    evacs.append((t, n, m0, cw))
        stage_total = []
        run = [0, 0]
        for e, (t, n, m0, w) in enumerate(evacs):
            both = m0 < 16 < m0 + w // P
            run[e % 2] += 32 if both else 16
            stage_total.append(run[e % 2])

        def in_use(K):
            if K < 0:
                return []
            if K < K_MIN:
                return [("w_in_used", K + 1 + CREDIT), ("w_out_used", K + 1 + CREDIT)]
            t = K - K_MIN
            if t < 8:
                got = [("qk_done", 3)] if t == 0 else [("kc_done", 2)] if t == 1 else \
                    [("vo_done", sum(1 for ev in evacs if ev[0] <= t))]
                return got + ([("unit_done", len(units)), ("state_ready", 8 * len(units))] if t == 7 else [])
            return [("gates_done", 1)] if K == K_GATE else [("mo_part", 8 * (K - K_MOUT + 1))]

        block = ctx.enter_context(nc.Block())

        @block.sync
        def _(sp):
            for dst, src in ((c_in, a["ccol"]), (prm, a["prm"]), (fcv, a["fcv"]), (ident, a["ident"]), (fold, a["fold"]),
                             (inv_x, a["inv_x"]), (inv_c, a["inv_c"]), (pool_w, a["pool_w"])):
                sp.dma_start(dst[:], src).then_inc(sem("const_in"), 16)
            sp.dma_start(in_c[:], a["ctx"]).then_inc(sem("ctx_in"), 16)
            sp.dma_start(y_x[:], a["x"]).then_inc(sem("x_in"), 16)
            for q in range(24):
                if q >= 4:
                    sp.wait_ge(sem("modw_used"), q - 3)
                sp.dma_start(modw[:, q % 4, :], a["modw"][q]).then_inc(sem(f"modw_in{q % 4}"), 16)

            def tile(K, src, slot):
                sp.wait_ge(sem("lo_in"), K + 1)
                sp.wait_ge(sem("lo_out"), K + 1)
                sp.dma_start(raw[:, slot, :], src).then_inc(sem(f"raw_in{slot}"), 16)

            def first_two(p):
                for j in range(2):
                    tile(p.k0 + j, a["ffn_w"][p.layer * FT + j], (p.k0 + j) % 2)

            def load_mod(c):
                sp.wait_ge(sem("modw1_used"), c)
                sp.dma_start(modw1[:], a["modw1"][c]).then_inc(sem("modw1_in"), 16)

            def the_rest(p):
                with sp.Fori(0, FT // 2 - 1) as i:
                    if p.index == 1:
                        load_mod(i + 1)
                    for e in range(2):
                        tile(i * 2 + (p.k0 + 2 + e), a["ffn_w"][i * 2 + (p.layer * FT + 2 + e)], (p.k0 + e) % 2)

            p0, p1, p2 = PASSES
            for j in range(2):
                sp.wait_ge(sem("modw_used"), 22 + j)
                tile(p0.k0 + j, a["ffn_w"][j], j)
            the_rest(p0)
            first_two(p1)
            sp.wait_ge(sem("w_in_used"), FT + CREDIT)
            sp.wait_ge(sem("x_out"), 16 * KT)
            sp.dma_start(res_x[:], x_scr[0]).then_inc(sem("res_in"), 16)
            sp.wait_ge(sem("hc_out"), 16)
            sp.dma_start(res_c[:], hc_scr).then_inc(sem("hc_in"), 16)
            sp.wait_ge(sem("post_done"), 8 * posts["x_ffn0"] + 8)
            sp.dma_start(modw1[:], a["modw1"][0]).then_inc(sem("modw1_in"), 16)
            the_rest(p1)
            load_mod(MODC - 1)
            sp.wait_ge(sem("hc_split"), 8)
            sp.wait_ge(sem("xc_out"), 16 * KT)
            sp.dma_start(res_c[:], xc_scr).then_inc(sem("resc_in"), 16)
            for t in range(12):
                K = K_MIN + t
                tile(K, a["mlstm_w"][t], K % 2)
                if K == K_GATE:
                    sp.wait_ge(sem("rows_ready"), 3)
                    for n, src in enumerate((gr, ga)):
                        sp.dma_start(row_scr[n], src[0:64, :]).then_inc(sem("rows_out"), 16)
                    sp.dma_start(al_scr, gend[0:64, 3, :]).then_inc(sem("rows_out"), 16)
                    sp.wait_ge(sem("rows_out"), 48)
                    for dr in range(2):
                        for par in range(2):
                            src = al_scr[32 * dr + par:32 * dr + 8:2, :]
                            sp.dma_start(alpha[64 * par:64 * par + 64, dr], src.unsqueeze(0).broadcast_to([64, 4, NCH]))\
                                .then_inc(sem("alpha_in"), 16)
                    sp.dma_start(masks[:], a["masks"]).then_inc(sem("mask_in"), 16)
                    sp.wait_ge(sem("cols_ready"), 4)
                    sp.wait_ge(sem("state_zero"), 2)
                    for i in range(2):
                        sp.wait_ge(sem(f"stage_out{i}"), run[i])
                    for u, (dr, n) in enumerate(units):
                        if n >= 2:
                            i = x_index[u]
                            if i >= 3:
                                sp.wait_ge(sem("num_done"), i - 2)
                            for par in range(2):
                                rows = slice(32 * dr + par, 32 * dr + 8, 2)
                                src = row_scr[0, rows, n * CH:n * CH + CH]
                                sp.dma_start(dmat[:, x_index[u] % 3, 4 * par:4 * par + 4, :],
                                             src.unsqueeze(0).broadcast_to([P, 4, CH])).then_inc(sem(f"row_in{i % 3}"), 16)
                                src = row_scr[1, rows, n * CH:n * CH + CH]
                                sp.dma_start(qa[64 * par:64 * par + 64, i % 3],
                                             src.unsqueeze(0).broadcast_to([64, 4, CH])).then_inc(sem(f"row_in{i % 3}"), 16)
                        if u >= 2:
                            sp.wait_ge(sem("unit_done"), u - 1)
                        sp.dma_start(vch[:, u % 2, :, 0:P], v_scr[n].rearrange("p (h v) -> p h v", v=P))\
                            .then_inc(sem(f"v_in{u % 2}"), 16)
                        if u in sec_index:
                            i = sec_index[u]
                            if i >= 2:
                                sp.wait_ge(sem("gated"), i - 1)
                            sp.dma_start(och[:, i % 2, :], o_scr[n - 2]).then_inc(sem(f"o_in{i % 2}"), 16)
            first_two(p2)
            sp.wait_ge(sem("mo_part"), 24)
            sp.wait_ge(sem("x_out"), 32 * KT)
            sp.dma_start(res_x[:], x_scr[1]).then_inc(sem("res_in"), 16)
            the_rest(p2)
            sp.wait_ge(sem("w_in_used"), 3 * FT + CREDIT)
            sp.wait_ge(sem("x_out"), 48 * KT)
            sp.dma_start(res_x[:], x_scr[0]).then_inc(sem("res_in"), 16)
            for d in range(KT):
                sp.wait_ge(sem("post_done"), 8 * posts["x_out"] + d + 1)
                sp.dma_start(a["out"][:, d, :], y_x[:, d, :]).then_inc(sem("out_done"), 16)
            sp.wait_ge(sem("out_done"), 16 * KT)

        @block.tensor
        def _(pe):
            def triple(out, whi, wlo, hhi, hlo, first, last):
                pe.matmul(out, whi, hhi, start=first, stop=False)
                pe.matmul(out, whi, hlo, start=False, stop=False)
                return pe.matmul(out, wlo, hhi, start=False, stop=last)

            def sums(key, T, k0=0, k1=KT):
                N, w = norms[key], T // 4
                if N >= 1 and k0 == 0:
                    pe.wait_ge(sem("std_ready"), N)
                for k in range(k0, k1):
                    pe.wait_ge(sem("sq_ready"), 8 * N + k + 1)
                    for g in range(4):
                        mm = pe.matmul(ps[32 * g:32 * g + 32, 1, 0:w], ones[:], sq[:, k % 2, g * w:g * w + w],
                                       start=(k == 0), stop=(k == KT - 1), tile_position=(0, 32 * g))
                    mm.then_inc(sem("sq_used"), 1)

            def spread(key, T):
                N, w = norms[key], T // 4
                pe.wait_ge(sem("rstd_ready"), N + 1)
                for g in range(4):
                    mm = pe.matmul(roots(T)[:, g * w:g * w + w], pick[:, g, :], rstd[N % 3][:, 0:w], start=True, stop=True)
                mm.then_inc(sem("r_ready"), 1)

            def norm(key, T):
                sums(key, T)
                spread(key, T)

            def mod_round(r, k0=0, k1=KT):
                for k in range(k0, k1):
                    q = KT * r + k
                    pe.wait_ge(sem(f"modw_in{q % 4}"), 16 * (q // 4 + 1))
                    for g in range(4):
                        mm = pe.matmul(ps[32 * g:32 * g + 32, 0, :], c_pad[:, k, :], modw[:, q % 4, 512 * g:512 * g + 512],
                                       start=(k == 0), stop=(k == KT - 1), tile_position=(0, 32 * g))
                    mm.then_inc(sem("modw_used"), 1)
                if k1 < KT:
                    return
                pe.wait_ge(sem("modrow_ready"), r + 1)
                if r >= 1:
                    pe.wait_ge(sem("mod_done"), r)
                for b in range(4):
                    mm = pe.transpose(ps[:, 2, P * b:P * b + P], modrow[:, P * b:P * b + P], ident[:])
                mm.then_inc(sem("modcol_ready"), 1)

            def mod_rows(c):
                pe.wait_ge(sem("modw1_in"), c * 16 + 16)
                if not isinstance(c, int) or c:
                    pe.wait_ge(sem("modrow1_ready"), c)
                for half in range(2):
                    for g in range(4):
                        mm = pe.matmul(ps[32 * g:32 * g + 32, 1, :], c_pad[:, 2 * g + half, :], modw1[:, 2 * g + half, :],
                                       start=(half == 0), stop=(half == 1), tile_position=(0, 32 * g))
                mm.then_inc(sem("modw1_used"), 1)

            def mod_columns(c):
                pe.wait_ge(sem("modrow1_ready"), c + 1)
                pe.wait_ge(sem("mod1_done"), c + 1)
                for b in range(4):
                    mm = pe.matmul(ps[:, 5, 2 * b:2 * b + 2], modrow1[:, P * b:P * b + P], fold[:], start=True, stop=True)
                mm.then_inc(sem("modcol1_ready"), 1)

            def mixer(s, g):
                src = mix_in_x if s == "x" else mix_in_c
                chunks, w = (2, 512) if s == "x" else (1, TC)
                first_in, first = (KT, KT) if s == "x" else (0, 0)
                pe.wait_ge(sem("mix_in_ready"), first_in + 2 * g + 2)
                for i in range(2 * g * chunks, 2 * (g + 1) * chunks):
                    mo, c = i // chunks % 2, i % chunks
                    if first + i >= 2:
                        pe.wait_ge(sem("mix_out_ready"), first + i - 1)
                    for ki in range(2):
                        mm = pe.matmul(ps[:, 4 + i % 2, 0:w], pool_w[:, g, ki, P * mo:P * mo + P],
                                       src[:, 2 * g + ki, c * w:c * w + w], start=(ki == 0), stop=(ki == 1))
                    mm.then_inc(sem("mix_done"), 1)

            def ffn(p, h_hi, h_lo, pre_base):
                def project_first():
                    s = p.k0 % 2
                    pe.wait_ge(sem("lo_in"), p.k0 + 1 + CREDIT)
                    if p.tap0:
                        pe.wait_ge(sem("tap_done"), p.tap0)
                        pe.wait_ge(sem("a_done"), p.j0)
                    for part in range(2):
                        for k in range(KT):
                            if pre_base is not None and part == 0:
                                pe.wait_ge(sem("pre_lo"), pre_base + k + 1)
                            for c in range(p.chunks):
                                cs = slice(c * p.cw, c * p.cw + p.cw)
                                ws = slice(1024 * part + P * k, 1024 * part + P * k + P)
                                mm = triple(ps[:, 2 * part + c, 0:p.cw], w_hi[:, s, ws], w_lo[:, s, ws],
                                            h_hi[:, k, cs], h_lo[:, k, cs], k == 0, k == KT - 1)
                        mm.then_inc(sem("g_done" if part == 0 else "w_in_used"), 1)

                def project_in(j, par):
                    s = (p.k0 + par) % 2
                    pe.wait_ge(sem("lo_in"), j + (p.k0 + 1 + CREDIT))
                    for part in range(2):
                        if part == 0:
                            pe.wait_ge(sem("tap_done"), j * len(p.taps) + p.tap0)
                        else:
                            pe.wait_ge(sem("a_done"), j + p.j0)
                        for c in range(p.chunks):
                            for k in range(KT):
                                cs = slice(c * p.cw, c * p.cw + p.cw)
                                ws = slice(1024 * part + P * k, 1024 * part + P * k + P)
                                mm = triple(ps[:, 2 * part + c, 0:p.cw], w_hi[:, s, ws], w_lo[:, s, ws],
                                            h_hi[:, k, cs], h_lo[:, k, cs], k == 0, k == KT - 1)
                        mm.then_inc(sem("g_done" if part == 0 else "w_in_used"), 1)

                def project_out(j, par):
                    s = (p.k0 + par) % 2
                    pe.wait_ge(sem("a_lo_ready"), j + (p.j0 + 1))
                    pe.wait_ge(sem("lo_out"), j + (p.k0 + 1 + CREDIT))
                    if p.chunks == 1:
                        for d in range(KT):
                            if d % 2 == 0:
                                pe.wait_ge(sem("y_added"), j * 8 + (8 * p.y0 + d + 6))
                            ws = slice(2048 + P * d, 2048 + P * d + P)
                            mm = triple(ps[:, 4 + 2 * (d // 2 % 2), p.cw * (d % 2):p.cw * (d % 2) + p.cw], w_hi[:, s, ws], w_lo[:, s, ws],
                                        a_hi[:, par, 0:p.cw], a_lo[:, par, 0:p.cw], True, True)
                            if d % 2 == 1:
                                mm.then_inc(sem("y_part" if d < 7 else "w_out_used"), 1)
                        return
                    for d in range(KT):
                        pe.wait_ge(sem("y_added"), j * 8 + (8 * p.y0 + d + 7))
                        ws = slice(2048 + P * d, 2048 + P * d + P)
                        for c in range(p.chunks):
                            cs = slice(c * p.cw, c * p.cw + p.cw)
                            mm = triple(ps[:, 4 + 2 * (d % 2) + c, 0:p.cw], w_hi[:, s, ws], w_lo[:, s, ws],
                                        a_hi[:, par, cs], a_lo[:, par, cs], True, True)
                        mm.then_inc(sem("y_part" if d < 7 else "w_out_used"), 1)

                with_mod = p.index == 1
                project_first()
                if with_mod:
                    mod_rows(0)
                with pe.Fori(0, FT // 2 - 1) as i:
                    project_in(i * 2 + 1, 1)
                    if with_mod:
                        mod_columns(i)
                        mod_rows(i + 1)
                    project_out(i * 2, 0)
                    project_in(i * 2 + 2, 0)
                    project_out(i * 2 + 1, 1)
                project_in(FT - 1, 1)
                if with_mod:
                    mod_columns(MODC - 2)
                    mod_rows(MODC - 1)
                project_out(FT - 2, 0)
                project_out(FT - 1, 1)
                if with_mod:
                    mod_columns(MODC - 1)

            pe.wait_ge(sem("const_in"), 8 * 16)
            pe.wait_ge(sem("ones_ready"), 1)
            pe.wait_ge(sem("pick_ready"), 4)
            pe.wait_ge(sem("cpad_ready"), 1)
            norm("c_in", TC)
            sums("x_in", TX)
            mod_round(0, 0, 3)
            spread("x_in", TX)
            mod_round(0, 3)
            for g in range(4):
                mod_round(1, g, g + 1)
                mixer("c", g)
            sums("c_mix", TC)
            mod_round(1, 4, 5)
            mixer("x", 0)
            mod_round(1, 5, 6)
            mixer("x", 1)
            mod_round(1, 6)
            spread("c_mix", TC)
            mod_round(2, 0, 3)
            mixer("x", 2)
            mod_round(2, 3)
            norm("c_pre2", TC)
            mixer("x", 3)
            norm("x_mix", TX)
            norm("x_pre2", TX)
            p0, p1, p2 = PASSES
            ffn(p0, hx_hi, hx_lo, 8 * splits["x_pre2"])
            norm("x_ffn0", TX)
            sums("x_pre1", TX)
            pe.wait_ge(sem("hc_split"), 8)
            ffn(p1, hc_hi, hc_lo, None)
            norm("c_ffn", TC)
            norm("c_pre1", TC)
            spread("x_pre1", TX)

            pe.wait_ge(sem("pre_lo"), 8 * splits["c_pre1"] + 8)
            e = 0
            for t in range(8):
                K = K_MIN + t
                s = K % 2
                pe.wait_ge(sem("lo_in"), K + 1 + CREDIT)
                pe.wait_ge(sem("lo_out"), K + 1 + CREDIT)

                def wcol(part, k, m0, n):
                    c0 = 384 * k + P * (m0 - 3 * t)
                    return (w_hi if part == 0 else w_lo)[:, s, c0:c0 + P * n]

                if t == 0:
                    for k in range(KT):
                        pe.wait_ge(sem("pre_lo"), 8 * splits["x_pre1"] + k + 1)
                        for c in range(2):
                            mm = triple(ps[:, c, :], wcol(0, k, 0, 1), wcol(1, k, 0, 1),
                                        hx_hi[:, k, 512 * c:512 * c + 512], hx_lo[:, k, 512 * c:512 * c + 512],
                                        k == 0, k == KT - 1)
                    mm.then_inc(sem("qk_done"), 1)
                for m in range(max(1, 3 * t), min(3 * t + 3, 8)):
                    if m >= 2:
                        pe.wait_ge(sem("qtap_done"), 8 * (m - 1))
                    for c in range(2):
                        for k in range(KT):
                            mm = triple(ps[:, 2 * (m % 2) + c, :], wcol(0, k, m, 1), wcol(1, k, m, 1),
                                        hx_hi[:, k, 512 * c:512 * c + 512], hx_lo[:, k, 512 * c:512 * c + 512],
                                        k == 0, k == KT - 1)
                    mm.then_inc(sem("qk_done"), 1)
                    if m >= 4:
                        if m >= 5:
                            pe.wait_ge(sem("kctap_done"), 2 * (m - 4))
                        for k in range(KT):
                            mm = triple(ps[:, 4, 0:TC], wcol(0, k, m, 1), wcol(1, k, m, 1), mc_hi[:, k, :], mc_lo[:, k, :],
                                        k == 0, k == KT - 1)
                        mm.then_inc(sem("kc_done"), 1)
                while e < len(evacs) and evacs[e][0] == t:
                    _, n, m0, w = evacs[e]
                    if e >= 3:
                        pe.wait_ge(sem("stage_ready"), e - 2)
                    hi, lo, t0 = (hx_hi, hx_lo, (n - 2) * CH) if n >= 2 else (mc_hi, mc_lo, n * CH)
                    out = ps[:, 5 + e % 3, 0:w]
                    for k in range(KT):
                        pe.matmul(out, hi[:, k, t0:t0 + CH], wcol(0, k, m0, w // P), start=(k == 0), stop=False)
                        pe.matmul(out, hi[:, k, t0:t0 + CH], wcol(1, k, m0, w // P), start=False, stop=False)
                        mm = pe.matmul(out, lo[:, k, t0:t0 + CH], wcol(0, k, m0, w // P), start=False, stop=(k == KT - 1))
                    mm.then_inc(sem("vo_done"), 1)
                    e += 1
            K, s = K_GATE, K_GATE % 2
            pe.wait_ge(sem("lo_in"), K + 1 + CREDIT)
            pe.wait_ge(sem("qtap_done"), 8 * 8)
            for part, (T, hi, lo) in enumerate(((512, hx_hi, hx_lo), (512, hx_hi, hx_lo), (TC, mc_hi, mc_lo))):
                t0 = 512 if part == 1 else 0
                for k in range(KT):
                    mm = triple(ps[:, part, 0:T], w_hi[:, s, P * k:P * k + P], w_lo[:, s, P * k:P * k + P],
                                hi[:, k, t0:t0 + T], lo[:, k, t0:t0 + T], k == 0, k == KT - 1)
            mm.then_inc(sem("gates_done"), 1)
            pe.wait_ge(sem("gates_ready"), 2)
            for n in range(NCH):
                for i, src in enumerate((gc_, gw, gem)):
                    b = 3 * n + i
                    mm = pe.transpose(ps[:, 4 + b // 8, 64 * (b % 8):64 * (b % 8) + 64], src[0:64, n * CH:n * CH + CH], ident[0:64, 0:64])
            mm.then_inc(sem("gcols_done"), 1)

            def k_tile(n, pair):
                return k_x[:, pair, (n - 2) * CH:(n - 1) * CH] if n >= 2 else k_c[:, pair, n * CH:(n + 1) * CH]

            def front(u):
                dr, n = units[u]
                if u >= 1:
                    pe.wait_ge(sem("kw_ready"), u)
                else:
                    pe.wait_ge(sem("cols_ready"), 4)
                for pair in range(4):
                    mm = pe.transpose(ps[:, 5, P * pair:P * pair + P], k_tile(n, pair), ident[:])
                mm.then_inc(sem("kt_done"), 1)
                if n >= 2:
                    i = x_index[u]
                    done = sum(1 for v in second if v <= u - 3)
                    if i >= 1:
                        pe.wait_ge(sem("sd_ready"), i)
                    if done:
                        pe.wait_ge(sem("glo_ready"), done)
                    for pair in range(4):
                        for par in range(2):
                            r = slice(64 * par, 64 * par + 64)
                            t = slice((n - 2) * CH, (n - 1) * CH)
                            mm = pe.matmul(ps[:, par, P * pair:P * pair + P], k_x[r, pair, t], q_x[r, pair, t],
                                           start=True, stop=True)
                    mm.then_inc(sem("s_done"), 1)

            def back(u):
                dr, n = units[u]
                pe.wait_ge(sem(f"v_in{u % 2}"), 16 * (u // 2 + 1))
                if n >= 2:
                    i = x_index[u]
                    pe.wait_ge(sem("sd_ready"), i + 1)
                    pe.wait_ge(sem("qa_ready"), i + 1)
                    if i >= 1:
                        pe.wait_ge(sem("hs_ready"), i)
                    pe.wait_ge(sem("state_ready"), 8 * (u - 1))
                    for h in range(HEADS):
                        pair, par = h // 2, h % 2
                        out = ps[:, 2 + h // 3, (P + 1) * (h % 3):(P + 1) * (h % 3 + 1)]
                        pe.matmul(out, dmat[:, x_index[u] % 3, 4 * par + pair, :], vch[:, u % 2, h, :], start=True, stop=False)
                        mm = pe.matmul(out, qa[:, x_index[u] % 3, pair, :], state[:, dr, h, :], start=False, stop=True)
                    mm.then_inc(sem("num_done"), 1)
                pe.wait_ge(sem("kw_ready"), u + 1)
                if u >= 1:
                    pe.wait_ge(sem("state_ready"), 8 * u)
                for h in range(HEADS):
                    pair, par = h // 2, h % 2
                    out = ps[64 * par:64 * par + 64, 6 + pair // 3, (P + 1) * (pair % 3):(P + 1) * (pair % 3 + 1)]
                    mm = pe.matmul(out, kw[:, u % 2, 64 * h:64 * h + 64], vch[:, u % 2, h, :], start=True, stop=True)
                mm.then_inc(sem("unit_done"), 1)

            def turn(u):
                if u not in sec_index:
                    return
                i = sec_index[u]
                pe.wait_ge(sem("gated"), i + 1)
                pe.wait_ge(sem("sd_ready"), sum(1 for v in x_units if v <= u + 2))
                if i >= 1:
                    pe.wait_ge(sem("glo_ready"), i)
                for h in range(HEADS):
                    mm = pe.transpose(ps[:, h // 4, P * (h % 4):P * (h % 4) + P], tmp[:, i % 2, P * h:P * h + P], ident[:])
                mm.then_inc(sem("turned"), 1)

            front(0)
            for u in range(len(units)):
                if u + 1 < len(units):
                    front(u + 1)
                back(u)
                if u >= 1:
                    turn(u - 1)
            turn(len(units) - 1)

            pe.wait_ge(sem("glo_ready"), 8)
            for t in range(3):
                K = K_MOUT + t
                s = K % 2
                ks = range(3 * t, min(3 * t + 3, KT))
                pe.wait_ge(sem("lo_in"), K + 1 + CREDIT)
                pe.wait_ge(sem("lo_out"), K + 1 + CREDIT)
                for d in range(KT):
                    pe.wait_ge(sem("y_added"), 8 * (2 * FT + t) + d + 7)
                    for c in range(2):
                        for k in ks:
                            ws = slice(1024 * (k - 3 * t) + P * d, 1024 * (k - 3 * t) + P * d + P)
                            gh, gl = g_hi[:, 4 * c:4 * c + 4, k, :], g_lo[:, 4 * c:4 * c + 4, k, :]
                            mm = triple(ps[:, 4 + 2 * (d % 2) + c, :], w_hi[:, s, ws], w_lo[:, s, ws], gh, gl,
                                        k == ks[0], k == ks[-1])
                    mm.then_inc(sem("mo_part"), 1)
            norm("x_mlstm", TX)
            norm("x_pre2b", TX)
            ffn(p2, hx_hi, hx_lo, 8 * splits["x_pre2b"])
            norm("x_out", TX)

        @block.scalar
        def _(act):
            own = [0]

            def chain(ins):
                own[0] += 1
                ins.then_inc(sem("act_own"), 1)

            def own_done():
                act.wait_ge(sem("act_own"), own[0])

            def norm(key, T, src, ready):
                N = norms[key]
                for k in range(KT):
                    ready(k)
                    act.wait_ge(sem("sq_used"), 8 * N + k + 1)
                    act.activation(sq[:, k % 2, 0:T], src(k), ACT.Square).then_inc(sem("sq_ready"), 1)
                act.wait_ge(sem("sq_used"), 8 * N + 8 + CREDIT)
                act.activation(rstd[N % 3][:, 0:T // 4], ssq(T), ACT.Sqrt, bias=prmc(PM_EPS), scale=1.0 / D)\
                    .then_inc(sem("std_ready"), 1)

            def mod_round(r):
                act.wait_ge(sem("modw_used"), KT * (r + 1))
                if r >= 1:
                    act.wait_ge(sem("modcol_ready"), r)
                act.activation(modrow[:], ps[:, 0, :], ACT.Copy).then_inc(sem("modrow_ready"), 1)
                act.wait_ge(sem("modcol_ready"), r + 1)
                view = ps[:, 2, :].rearrange("p (b g x) -> p g b x", b=4, g=4)
                for s in range(2):
                    ins = act.activation(modt[:, s, 16 * r:16 * r + 16].rearrange("p (g b) -> p g b", b=4),
                                         view[:, :, :, s], ACT.Copy)
                ins.then_inc(sem("mod_done"), 1)

            def mixer(s, g):
                src, dst = (mix_in_x, mix_out_x) if s == "x" else (mix_in_c, mix_out_c)
                chunks, w = (2, 512) if s == "x" else (1, TC)
                first = KT if s == "x" else 0
                for k in (2 * g, 2 * g + 1):
                    act.wait_ge(sem("pooled"), first + k + 1)
                    act.activation(src[:, k, :], src[:, k, :], ACT.Copy, scale=derived(0, 0, s, k)).then_inc(sem("mix_in_ready"), 1)
                for i in range(2 * g * chunks, 2 * (g + 1) * chunks):
                    d, c = i // chunks, i % chunks
                    act.wait_ge(sem("mix_done"), first + i + 1)
                    act.activation(dst[:, d, c * w:c * w + w], ps[:, 4 + i % 2, 0:w], ACT.Copy, scale=prmc(PM_PS + d))\
                        .then_inc(sem("mix_out_ready"), 1)

            def norm_mix(s):
                dst, first, chunks = (mix_out_x, KT, 2) if s == "x" else (mix_out_c, 0, 1)
                norm(f"{s}_mix", TOK[s], lambda k: dst[:, k, :],
                     lambda k: act.wait_ge(sem("mix_out_ready"), first + chunks * (k + 1)))

            def norm_pre(key, s, src, post, dst=None, counter=None):
                def ready(k):
                    act.wait_ge(sem("post_done"), 8 * post + k + 1)
                    if dst is not None:
                        act.dma_start(dst[:, k, :], src[:, k, :]).then_inc(sem(counter), 16)
                norm(key, TOK[s], lambda k: src[:, k, :], ready)

            def pre_hi(key, s, layer, which, src, dst, k0=0, k1=KT):
                n = pres[key]
                for k in range(k0, k1):
                    act.wait_ge(sem("pre_t"), 8 * n + k + 1)
                    act.activation(dst[:, k, :], src[:, k, :], ACT.Identity, bias=shift(layer, which, s, k))\
                        .then_inc(sem("pre_hi"), 1)

            def hi_in(turn, used, slot):
                act.wait_ge(sem(f"raw_in{slot}"), turn)
                act.wait_ge(sem("w_in_used"), used)
                act.activation(w_hi[:, slot, 0:2048], raw[:, slot, 0:2048], ACT.Copy).then_inc(sem("hi_done"), 1)

            def hi_out(used, slot):
                act.wait_ge(sem("w_out_used"), used)
                act.activation(w_hi[:, slot, 2048:WT], raw[:, slot, 2048:WT], ACT.Copy).then_inc(sem("hi_done"), 1)

            def hi_tile(K):
                slot = K % 2
                act.wait_ge(sem(f"raw_in{slot}"), 16 * (K // 2 + 1))
                for name, count in in_use(K - 2):
                    act.wait_ge(sem(name), count)
                act.activation(w_hi[:, slot, 0:2048], raw[:, slot, 0:2048], ACT.Copy).then_inc(sem("hi_done"), 1)
                act.activation(w_hi[:, slot, 2048:WT], raw[:, slot, 2048:WT], ACT.Copy).then_inc(sem("hi_done"), 1)

            def ffn(p):
                def tile(j, par, last=False):
                    act.wait_ge(sem("g_done"), j + (p.j0 + 1))
                    if not (isinstance(j, int) and j + p.j0 == 0):
                        act.wait_ge(sem("a_done"), j + p.j0)
                    cv = fcv[:, j + p.layer * FT, :] if not isinstance(j, int) else fcv[:, p.layer * FT + j, :]
                    act.activation(acc[:, 0:p.T], bank(0, p.T), ACT.Identity, bias=cv[:, 9:10], scale=cv[:, 4:5])\
                        .then_inc(sem("acc_ready"), 1)
                    s = (p.k0 + par + 1) % 2
                    if not last:
                        c = (p.k0 + par + 1) // 2 + 1
                        turn = (j - par) * 8 + 16 * c if not isinstance(j, int) else 16 * ((p.k0 + j + 1) // 2 + 1)
                        hi_in(turn, j + (p.j0 + 2), s)
                    act.wait_ge(sem("tap_done"), j * len(p.taps) + (p.tap0 + len(p.taps)))
                    act.activation(acc[:, 0:p.T], acc[:, 0:p.T], ACT.Silu).then_inc(sem("silu_done"), 1)
                    act.wait_ge(sem("a_done"), j + (p.j0 + 1))
                    act.wait_ge(sem("w_out_used"), j + (p.j0 + 1))
                    act.activation(a_hi[:, par, 0:p.T], prod[:, 0:p.T], ACT.Copy).then_inc(sem("a_hi_ready"), 1)
                    if not last:
                        hi_out(j + (p.j0 + 2), s)

                def mod_rows(c):
                    act.wait_ge(sem("modw1_used"), c + 1)
                    if not isinstance(c, int) or c:
                        act.wait_ge(sem("modcol1_ready"), c)
                    act.activation(modrow1[:], ps[:, 1, :], ACT.Copy).then_inc(sem("modrow1_ready"), 1)

                def mod_columns(c):
                    act.wait_ge(sem("modcol1_ready"), c + 1)
                    act.activation(modt[:].rearrange("p s (c b) -> p s c b", b=4)[:, :, c + MODC, :], ps[:, 5, 0:8].rearrange("p (b x) -> p x b", x=2), ACT.Copy)\
                        .then_inc(sem("mod1_done"), 1)

                with_mod = p.index == 1
                tile(0, 0)
                if with_mod:
                    mod_rows(0)
                with act.Fori(0, FT // 2 - 1) as i:
                    tile(i * 2 + 1, 1)
                    if with_mod:
                        mod_columns(i)
                        mod_rows(i + 1)
                    tile(i * 2 + 2, 0)
                tile(FT - 1, 1, True)
                if with_mod:
                    mod_columns(MODC - 2)
                    mod_rows(MODC - 1)
                    mod_columns(MODC - 1)

            p0, p1, p2 = PASSES
            act.wait_ge(sem("const_in"), 8 * 16)
            act.wait_ge(sem("cpad_zero"), 1)
            act.activation(c_pad[:, :, 0:2], c_in[:], ACT.Silu).then_inc(sem("cpad_ready"), 1)
            norm("c_in", TC, lambda k: in_c[:, k, :], lambda k: act.wait_ge(sem("ctx_in"), 16))
            norm("x_in", TX, lambda k: y_x[:, k, :], lambda k: act.wait_ge(sem("x_in"), 16))
            mod_round(0)
            act.wait_ge(sem("derived"), 1)
            for g in range(4):
                mixer("c", g)
            norm_mix("c")
            mixer("x", 0)
            mixer("x", 1)
            mod_round(1)
            mixer("x", 2)
            mod_round(2)
            norm_pre("c_pre2", "c", in_c, posts["c_mix"], xc_scr, "xc_out")
            mixer("x", 3)
            for k in range(KT):
                act.wait_ge(sem("pre_t"), k + 1)
                act.activation(mix_in_c[:, k, :], mix_in_c[:, k, :], ACT.Identity, bias=shift(0, 1, "c", k)).then_inc(sem("pre_hi"), 1)
            act.wait_ge(sem("pre_hi"), 8)
            act.dma_start(hc_scr, mix_in_c[:]).then_inc(sem("hc_out"), 16)
            norm_mix("x")
            norm_pre("x_pre2", "x", y_x, posts["x_mix"], x_scr[0], "x_out")
            act.wait_ge(sem("hc_out"), 16)
            act.wait_ge(sem("xc_out"), 16 * KT)
            hi_tile(p0.k0)
            pre_hi("x_pre2", "x", 0, 1, y_x, hx_hi)
            ffn(p0)
            hi_tile(p1.k0)
            norm("x_ffn0", TX, lambda k: y_x[:, k, :], lambda k: act.wait_ge(sem("y_added"), 8 * (p0.y0 + FT) + k + 1))
            norm_pre("x_pre1", "x", y_x, posts["x_ffn0"], x_scr[1], "x_out")
            act.wait_ge(sem("hc_in"), 16)
            act.wait_ge(sem("w_in_used"), FT + CREDIT)
            for k in range(KT):
                act.activation(hc_hi[:, k, :], res_c[:, k, :], ACT.Copy).then_inc(sem("hc_hi"), 1)
            ffn(p1)
            hi_tile(K_MIN)
            norm("c_ffn", TC, lambda k: y_c[:, k, :], lambda k: act.wait_ge(sem("y_added"), 8 * (p1.y0 + FT) + k + 1))
            norm_pre("c_pre1", "c", y_c, posts["c_ffn"])
            pre_hi("c_pre1", "c", 1, 0, y_c, mc_hi)
            pre_hi("x_pre1", "x", 1, 0, y_x, hx_hi)

            e = 0
            for t in range(8):
                hi_tile(K_MIN + t + 1)
                for m in range(3 * t, min(3 * t + 3, 8)):
                    cv = prm[:, PM_MCV + 10 * m:PM_MCV + 10 * m + 10]
                    dst = q_x[:, m, :] if m < 4 else k_x[:, m - 4, :]
                    act.wait_ge(sem("qk_done"), m + 1)
                    if m >= 1:
                        own_done()
                    act.activation(acc[:], bank(2 * (m % 2), TX), ACT.Identity, bias=cv[:, 9:10], scale=cv[:, 4:5])\
                        .then_inc(sem("qacc_ready"), 1)
                    if m >= 4:
                        act.wait_ge(sem("kc_done"), m - 3)
                        act.activation(acc_c[:], ps[:, 4, 0:TC], ACT.Identity, bias=cv[:, 9:10], scale=cv[:, 4:5])\
                            .then_inc(sem("kcacc_ready"), 1)
                    act.wait_ge(sem("qtap_done"), 8 * (m + 1))
                    if m == 0:
                        act.wait_ge(sem("pre_lo"), 8 * splits["x_pre1"] + 8)
                    chain(act.activation(dst, acc[:], ACT.Silu))
                    if m >= 4:
                        own_done()
                        chain(act.activation(dst, dst, ACT.Copy, scale=0.125))
                        act.wait_ge(sem("kctap_done"), 2 * (m - 3))
                        chain(act.activation(k_c[:, m - 4, :], acc_c[:], ACT.Silu))
                        own_done()
                        chain(act.activation(k_c[:, m - 4, :], k_c[:, m - 4, :], ACT.Copy, scale=0.125))
                        own_done()
                while e < len(evacs) and evacs[e][0] == t:
                    _, n, m0, w = evacs[e]
                    act.wait_ge(sem("vo_done"), e + 1)
                    if e >= 2:
                        act.wait_ge(sem(f"stage_out{e % 2}"), stage_total[e - 2])
                    nv = max(0, min(16 - m0, w // P)) * P
                    out = ps[:, 5 + e % 3, 0:w]
                    if nv:
                        ins = act.activation(stage[:, e % 2, 0:nv], out[:, 0:nv], ACT.Copy)
                    if w > nv:
                        ins = act.activation(stage[:, e % 2, nv:w], out[:, nv:w], ACT.Sigmoid)
                    ins.then_inc(sem("stage_ready"), 1)
                    act.wait_ge(sem("stage_ready"), e + 1)
                    if nv:
                        act.dma_start(v_scr[n, :, P * (m0 - 8):P * (m0 - 8) + nv], stage[:, e % 2, 0:nv])\
                            .then_inc(sem(f"stage_out{e % 2}"), 16)
                    if w > nv:
                        c0 = P * (max(m0, 16) - 16)
                        act.dma_start(o_scr[n - 2, :, c0:c0 + w - nv], stage[:, e % 2, nv:w])\
                            .then_inc(sem(f"stage_out{e % 2}"), 16)
                    e += 1
            act.wait_ge(sem("gates_done"), 1)
            chain(act.activation(gates[:, TC:TC + TX], bank(0, TX), ACT.Identity, bias=prmc(PM_GB)))
            chain(act.activation(gates[:, 0:TC], ps[:, 2, 0:TC], ACT.Identity, bias=prmc(PM_GB)))
            own_done()
            f = slice(64, P)
            chain(act.activation(gtmp[f, :], gates[f, :], ACT.Abs))
            own_done()
            chain(act.activation(gtmp[f, :], gtmp[f, :], ACT.Exp, scale=-1.0))
            own_done()
            act.activation(gtmp[f, :], gtmp[f, :], ACT.Ln, bias=1.0).then_inc(sem("softplus"), 1)
            r64 = slice(0, 64)
            act.wait_ge(sem("gexp_in"), 1)
            act.activation(gw[r64, :], gw[r64, :], ACT.Exp).then_inc(sem("gates_ready"), 1)
            act.activation(gem[r64, :], gmax[r64, :], ACT.Exp, scale=-1.0).then_inc(sem("gates_ready"), 1)
            act.activation(ga[r64, :], ga[r64, :], ACT.Exp).then_inc(sem("rows_ready"), 1)
            act.activation(gend[r64, 3, :], gend[r64, 3, :], ACT.Exp).then_inc(sem("rows_ready"), 1)
            act.wait_ge(sem("gcols_done"), 1)
            flat = cols[:].rearrange("p n i r -> p (n i r)")
            for b in range(4):
                w = min(512, 64 * 3 * NCH - 512 * b)
                act.activation(flat[:, 512 * b:512 * b + w], ps[:, 4 + b, 0:w], ACT.Copy).then_inc(sem("cols_ready"), 1)

            def turned(u):
                if u in sec_index:
                    i, c = sec_index[u], units[u][1] - 2
                    act.wait_ge(sem("turned"), i + 1)
                    act.activation(g_hi[:, c, :, :].rearrange("p h t -> p (h t)"), bank(0, 1024), ACT.Copy).then_inc(sem("ghi_ready"), 1)

            def decay(u):
                if u in x_index:
                    act.wait_ge(sem("dexp_ready"), x_index[u] + 1)
                    act.activation(dmat[:, x_index[u] % 3], dmat[:, x_index[u] % 3], ACT.Exp).then_inc(sem("d_ready"), 1)

            decay(0)
            for u in range(len(units)):
                if u + 1 < len(units):
                    decay(u + 1)
                if u >= 1:
                    turned(u - 1)
            turned(len(units) - 1)
            for t in range(3):
                hi_tile(K_MOUT + t)
            hi_tile(p2.k0)
            norm("x_mlstm", TX, lambda k: y_x[:, k, :], lambda k: act.wait_ge(sem("y_added"), 8 * (2 * FT + 3) + k + 1))
            norm_pre("x_pre2b", "x", y_x, posts["x_mlstm"], x_scr[0], "x_out")
            pre_hi("x_pre2b", "x", 1, 1, y_x, hx_hi)
            ffn(p2)
            norm("x_out", TX, lambda k: y_x[:, k, :], lambda k: act.wait_ge(sem("y_added"), 8 * (p2.y0 + FT) + k + 1))

        @block.vector
        def _(dve):
            own = [0]

            def chain(ins):
                own[0] += 1
                ins.then_inc(sem("dve_own"), 1)

            def own_done():
                dve.wait_ge(sem("dve_own"), own[0])

            early = []

            def root(key, T):
                N = norms[key]
                dve.wait_ge(sem("std_ready"), N + 1)
                early.append(key)
                dve.reciprocal(rstd[N % 3][:, 0:T // 4], rstd[N % 3][:, 0:T // 4]).then_inc(sem("rstd_ready"), 1)

            def norm(key, T):
                if key not in early:
                    root(key, T)
                dve.wait_ge(sem("r_ready"), spreads[key] + 1)
                return roots(T)

            def pool(s, src, dst, k0=0, k1=KT):
                T = TOK[s]
                R, W = GRID[s]
                Wp = W + 2 * PAD
                r = norm(f"{s}_in", T) if k0 == 0 else roots(T)
                z = zpad[:, 0:R * Wp].rearrange("p (r w) -> p r w", w=Wp)
                bufs = [b[:, 0:R * Wp].rearrange("p (r w) -> p r w", w=Wp) for b in (sum_a, sum_b)]
                inv = inv_x if s == "x" else inv_c
                if k0 == 0:
                    chain(dve.memset(zpad[:], 0.0))
                for k in range(k0, k1):
                    own_done()
                    chain(dve.tensor_tensor(z[:, :, PAD:PAD + W], grid(src[:, k, :], s), grid(r, s), ALU.mult))
                    own_done()
                    levels = k // 2 + 1
                    reach = [sum(2 ** (i - 1) for i in range(lv + 1, levels) if i >= 1) for lv in range(levels)]
                    cur = z
                    for lv in range(levels):
                        lo, hi = PAD - reach[lv], PAD + W + reach[lv]
                        back, fwd = (1, 0) if lv == 0 else (2 ** (lv - 1), 2 ** (lv - 1))
                        out = bufs[lv % 2]
                        chain(dve.tensor_tensor(out[:, :, lo:hi], cur[:, :, lo - back:hi - back],
                                                cur[:, :, lo + fwd:hi + fwd], ALU.add))
                        own_done()
                        cur = out
                    other = bufs[levels % 2]
                    weights = inv[:, k // 2, :].unsqueeze(1).broadcast_to([P, R, W])
                    chain(dve.tensor_tensor(other[:, :, PAD:PAD + W], cur[:, :, PAD:PAD + W], weights, ALU.mult))
                    own_done()
                    dve.tensor_tensor(grid(dst[:, k, :], s), other[:, :, PAD:PAD + W], z[:, :, PAD:PAD + W], ALU.subtract)\
                        .then_inc(sem("pooled"), 1)
                    dve.wait_ge(sem("pooled"), (0 if s == "c" else KT) + k + 1)

            def derive(layer, r0, r1, count):
                if layer == 0:
                    dve.wait_ge(sem("mod_done"), r1)
                else:
                    dve.wait_ge(sem("mod1_done"), MODC + 1)
                c0, c1 = 48 * layer + 16 * r0, 48 * layer + 16 * r1
                for s in range(2):
                    chain(dve.tensor_tensor(modt[:, s, c0:c1], modt[:, s, c0:c1], prm[:, PM_MODB + c0:PM_MODB + c1], ALU.add))
                own_done()
                for s in ("x", "c"):
                    for i, sec in enumerate((1, 2, 4, 5)):
                        if not r0 <= sec // 2 < r1:
                            continue
                        g = prm[:, PM_G + 32 * layer + 8 * i:PM_G + 32 * layer + 8 * i + 8]
                        out = der[:, layer, 0 if s == "x" else 1, i, :]
                        if i % 2 == 0:
                            ins = dve.scalar_tensor_tensor(out, mod(layer, sec, s), 1.0, g, ALU.add, ALU.mult)
                        else:
                            ins = dve.tensor_tensor(out, mod(layer, sec, s), g, ALU.mult)
                ins.then_inc(sem("derived"), 1)
                dve.wait_ge(sem("derived"), count)

            def post(key, s, layer, which, y, x, out, ready=None):
                r = norm(key, TOK[s])
                for d in range(KT + 1):
                    if d < KT:
                        chain(dve.scalar_tensor_tensor(y[:, d, :], y[:, d, :], derived(layer, which, s, d), r, ALU.mult, ALU.mult))
                    if d >= 1:
                        if d == 1 and ready is not None:
                            ready()
                        dve.wait_ge(sem("dve_own"), own[0] - (1 if d < KT else 0))
                        dve.tensor_tensor(out[:, d - 1, :], y[:, d - 1, :], x[:, d - 1, :], ALU.add).then_inc(sem("post_done"), 1)

            def pre(key, s, layer, which, src, hi=None, lo=None, stored=None, dst=None):
                n = pres[key]
                r = norm(key, TOK[s])
                if stored is not None:
                    dve.wait_ge(sem(stored[0]), stored[1])
                for d in range(KT + 1):
                    if d < KT:
                        dve.scalar_tensor_tensor((src if dst is None else dst)[:, d, :], src[:, d, :], derived(layer, which, s, d), r,
                                                 ALU.mult, ALU.mult).then_inc(sem("pre_t"), 1)
                    if d >= 1 and lo is not None:
                        dve.wait_ge(sem("pre_hi"), 8 * n + d)
                        dve.scalar_tensor_tensor(lo[:, d - 1, :], src[:, d - 1, :], shift(layer, which // 2, s, d - 1),
                                                 hi[:, d - 1, :].bitcast(F32), ALU.add, ALU.subtract).then_inc(sem("pre_lo"), 1)

            def lo_out(count, slot):
                dve.wait_ge(sem("hi_done"), count)
                dve.tensor_tensor(w_lo[:, slot, 2048:WT], raw[:, slot, 2048:WT], w_hi[:, slot, 2048:WT].bitcast(F32), ALU.subtract)\
                    .then_inc(sem("lo_out"), 1)

            def lo_tile(K):
                lo_out(2 * K + 2, K % 2)

            def ffn(p, y):
                NTAP = len(p.taps)

                def conv(j, par):
                    s = (p.k0 + par) % 2
                    lo_out(j * 2 + (2 * p.k0 + 2), s)
                    cv = fcv[:, j + p.layer * FT, :]
                    g, ac = grid(bank(0, p.T), p.stream), grid(acc[:, 0:p.T], p.stream)
                    dve.wait_ge(sem("acc_ready"), j + (p.j0 + 1))
                    for i, (r, c) in enumerate(p.taps):
                        out, src = tap_views(ac, g, r, c, p.R, p.W)
                        if i:
                            dve.wait_ge(sem("tap_done"), j * NTAP + (p.tap0 + i))
                        t = tap_index(r, c)
                        dve.scalar_tensor_tensor(out, src, cv[:, t:t + 1], out, ALU.mult, ALU.add).then_inc(sem("tap_done"), 1)

                def gate(j):
                    dve.wait_ge(sem("silu_done"), j + (p.j0 + 1))
                    dve.wait_ge(sem("w_in_used"), j + (p.j0 + 1 + CREDIT))
                    if not (isinstance(j, int) and j + p.j0 == 0):
                        dve.wait_ge(sem("a_lo_ready"), j + p.j0)
                    dve.tensor_tensor(prod[:, 0:p.T], acc[:, 0:p.T], bank(2, p.T), ALU.mult).then_inc(sem("a_done"), 1)

                def add(j, par):
                    if p.chunks == 1:
                        for d in range(0, KT, 2):
                            if d < 6:
                                dve.wait_ge(sem("y_part"), j * 3 + (p.parts0 + d // 2 + 1))
                            else:
                                dve.wait_ge(sem("w_out_used"), j + (p.j0 + 1 + CREDIT))
                            dve.wait_ge(sem("y_added"), j * 8 + (8 * p.y0 + d + 2))
                            out = y[:, d:d + 2, :].rearrange("p d t -> p (d t)")
                            dve.tensor_tensor(out, out, ps[:, 4 + 2 * (d // 2 % 2), :], ALU.add).then_inc(sem("y_added"), 2)
                        return
                    for d in range(KT):
                        if d < 7:
                            dve.wait_ge(sem("y_part"), j * 7 + (p.parts0 + d + 1))
                        else:
                            dve.wait_ge(sem("w_out_used"), j + (p.j0 + 1 + CREDIT))
                        dve.wait_ge(sem("y_added"), j * 8 + (8 * p.y0 + d + 1))
                        dve.tensor_tensor(y[:, d, :], y[:, d, :], bank(4 + 2 * (d % 2), p.T), ALU.add).then_inc(sem("y_added"), 1)

                conv(0, 0)
                gate(0)
                dve.wait_ge(sem("y_zero"), p.index + 1)
                with dve.Fori(0, FT // 2 - 1) as i:
                    conv(i * 2 + 1, 1)
                    add(i * 2, 0)
                    gate(i * 2 + 1)
                    conv(i * 2 + 2, 0)
                    add(i * 2 + 1, 1)
                    gate(i * 2 + 2)
                conv(FT - 1, 1)
                add(FT - 2, 0)
                gate(FT - 1)
                add(FT - 1, 1)

            p0, p1, p2 = PASSES
            for name, n in (("sq_used", 2), ("w_in_used", 2), ("w_out_used", 2), ("lo_in", 2), ("lo_out", 2), ("y_added", 8), ("mod1_done", 1)):
                dve.sem_inc(sem(name), n)
            dve.memset(ones[:], 1.0).then_inc(sem("ones_ready"), 1)
            chain(dve.memset(pick[:], 0.0))
            own_done()
            for g in range(4):
                dve.memset(pick[32 * g:32 * g + 1, g, :], 1.0).then_inc(sem("pick_ready"), 1)
            dve.memset(c_pad[:], 0.0).then_inc(sem("cpad_zero"), 1)
            dve.wait_ge(sem("const_in"), 8 * 16)
            pool("c", in_c, mix_in_c, 0, 5)
            root("x_in", TX)
            pool("c", in_c, mix_in_c, 5, 8)
            pool("x", y_x, mix_in_x, 0, 2)
            derive(0, 0, 1, 1)
            pool("x", y_x, mix_in_x, 2, 5)
            root("c_mix", TC)
            pool("x", y_x, mix_in_x, 5, 6)
            derive(0, 1, 2, 2)
            post("c_mix", "c", 0, 1, mix_out_c, in_c, in_c)
            pool("x", y_x, mix_in_x, 6, 7)
            root("c_pre2", TC)
            pool("x", y_x, mix_in_x, 7, 8)
            derive(0, 2, 3, 3)
            pre("c_pre2", "c", 0, 2, in_c, dst=mix_in_c)
            post("x_mix", "x", 0, 1, mix_out_x, y_x, y_x)
            pre("x_pre2", "x", 0, 2, y_x, hx_hi, hx_lo, ("x_out", 16 * KT))
            ffn(p0, y_x)
            post("x_ffn0", "x", 0, 3, y_x, res_x, y_x, lambda: dve.wait_ge(sem("res_in"), 16))
            root("x_pre1", TX)
            ffn(p1, y_c)
            post("c_ffn", "c", 0, 3, y_c, res_c, y_c, lambda: dve.wait_ge(sem("resc_in"), 16))
            derive(1, 0, 3, 4)
            pre("c_pre1", "c", 1, 0, y_c, mc_hi, mc_lo)
            dve.wait_ge(sem("pre_lo"), 8 * splits["c_pre1"] + 8)
            pre("x_pre1", "x", 1, 0, y_x, hx_hi, hx_lo, ("x_out", 32 * KT))
            lo_tile(K_MIN)

            for t in range(8):
                lo_tile(K_MIN + t + 1)
                for m in range(3 * t, min(3 * t + 3, 8)):
                    cv = prm[:, PM_MCV + 10 * m:PM_MCV + 10 * m + 10]
                    dve.wait_ge(sem("qacc_ready"), m + 1)
                    for i, (r, c) in enumerate(taps_of("x")):
                        out, src = tap_views(grid(acc[:], "x"), grid(bank(2 * (m % 2), TX), "x"), r, c, *GRID["x"])
                        if i:
                            dve.wait_ge(sem("qtap_done"), 8 * m + i)
                        tt = tap_index(r, c)
                        dve.scalar_tensor_tensor(out, src, cv[:, tt:tt + 1], out, ALU.mult, ALU.add).then_inc(sem("qtap_done"), 1)
                    if m >= 4:
                        dve.wait_ge(sem("kcacc_ready"), m - 3)
                        for i, (r, c) in enumerate(taps_of("c")):
                            out, src = tap_views(grid(acc_c[:], "c"), grid(ps[:, 4, 0:TC], "c"), r, c, *GRID["c"])
                            if i:
                                dve.wait_ge(sem("kctap_done"), 2 * (m - 4) + i)
                            tt = tap_index(r, c)
                            dve.scalar_tensor_tensor(out, src, cv[:, tt:tt + 1], out, ALU.mult, ALU.add).then_inc(sem("kctap_done"), 1)

            f64 = slice(64, P)
            r64 = slice(0, 64)
            fw, bw = slice(0, 8), slice(32, 40)
            dve.wait_ge(sem("gates_done"), 1)
            dve.wait_ge(sem("lo_out"), K_GATE + 1 + CREDIT)
            for t_ in (gcum, gmax):
                chain(dve.memset(t_[r64, :], 0.0))
            chain(dve.memset(greset[r64, :], 1.0))
            chain(dve.memset(gend[r64], 0.0))
            own_done()
            r3 = greset[:].rearrange("p (n t) -> p n t", t=CH)
            chain(dve.memset(r3[0:32, :, 0:1], 0.0))
            chain(dve.memset(r3[32:64, :, CH - 1:CH], 0.0))
            dve.wait_ge(sem("softplus"), 1)
            chain(dve.scalar_tensor_tensor(logf[r64, :], gates[f64, :], 0.0, gtmp[f64, :], ALU.min, ALU.subtract))
            own_done()
            chain(dve.tensor_tensor_scan(gcum[fw, :], greset[fw, :], logf[fw, :], 0.0, ALU.mult, ALU.add))
            chain(dve.tensor_tensor_scan(gcum[bw, :][:, ::-1], greset[bw, :][:, ::-1], logf[bw, :][:, ::-1], 0.0, ALU.mult, ALU.add))
            chain(dve.tensor_tensor_scan(gmax[fw, :], logf[fw, :], gates[fw, :], 0.0, ALU.add, ALU.max))
            chain(dve.tensor_tensor_scan(gmax[bw, 0:TC][:, ::-1], logf[bw, 0:TC][:, ::-1], gates[bw, 0:TC][:, ::-1], 0.0,
                                         ALU.add, ALU.max))
            own_done()
            chain(dve.tensor_tensor_scan(gmax[bw, TC:NT][:, ::-1], logf[bw, TC:NT][:, ::-1], gates[bw, TC:NT][:, ::-1],
                                         gmax[bw, 0:1], ALU.add, ALU.max))
            own_done()
            b3 = gcum[:].rearrange("p (n t) -> p n t", t=CH)
            m3 = gmax[:].rearrange("p (n t) -> p n t", t=CH)
            f, b = slice(0, 32), slice(32, 64)
            chain(dve.tensor_copy(gend[f, 0, 1:NCH], m3[f, 0:NCH - 1, CH - 1]))
            chain(dve.tensor_copy(gend[b, 0, 2:NCH - 1], m3[b, 3:NCH, 0]))
            chain(dve.tensor_copy(gend[b, 0, NCH - 1:NCH], m3[b, 0, 0:1]))
            chain(dve.tensor_copy(gend[b, 0, 0:1], m3[b, 1, 0:1]))
            chain(dve.tensor_tensor(gend[f, 1, :], b3[f, :, CH - 1], m3[f, :, CH - 1], ALU.subtract))
            chain(dve.tensor_tensor(gend[b, 1, :], b3[b, :, 0], m3[b, :, 0], ALU.subtract))
            chain(dve.tensor_tensor(gc_[r64, :], gates[r64, :], gcum[r64, :], ALU.subtract))
            dve.tensor_tensor(gr[r64, :], gcum[r64, :], gmax[r64, :], ALU.subtract).then_inc(sem("rows_ready"), 1)
            own_done()
            dve.wait_ge(sem("rows_ready"), 1)

            def spread(i):
                return gend[r64, i, :].unsqueeze(2).broadcast_to([64, NCH, CH])

            def chunks(t_):
                return t_[r64, :].rearrange("p (n t) -> p n t", t=CH)

            chain(dve.tensor_tensor(gend[r64, 3, :], gend[r64, 0, :], gend[r64, 1, :], ALU.add))
            chain(dve.tensor_tensor(chunks(ga), chunks(gr), spread(0), ALU.add))
            dve.tensor_tensor(chunks(gw), chunks(gc_), spread(1), ALU.add).then_inc(sem("gexp_in"), 1)
            own_done()
            dve.wait_ge(sem("cols_ready"), 4)
            dve.wait_ge(sem("rows_out"), 48)
            dve.memset(state[:], 0.0).then_inc(sem("state_zero"), 1)
            dve.memset(vch[:, :, :, P:P + 1], 1.0).then_inc(sem("state_zero"), 1)
            dve.wait_ge(sem("state_zero"), 2)
            dve.wait_ge(sem("alpha_in"), 64)

            def col(n, i, dr):
                return cols[:, n, i, 32 * dr:32 * dr + 8]

            def front(u):
                dr, n = units[u]
                dve.wait_ge(sem("kt_done"), u + 1)
                if u >= 2:
                    dve.wait_ge(sem("unit_done"), u - 1)
                dve.tensor_tensor(kw[:, u % 2, :].rearrange("p (h k) -> p h k", k=64), ps[:, 5, :].rearrange("p (h k) -> p h k", k=64),
                                  col(n, 1, dr).unsqueeze(2).broadcast_to([P, HEADS, 64]), ALU.mult).then_inc(sem("kw_ready"), 1)
                if n >= 2:
                    i = x_index[u]
                    dve.wait_ge(sem("masked"), i + 1)
                    dm = dmat[:, x_index[u] % 3].rearrange("p (a b) t -> p a b t", a=2)
                    cc = col(n, 0, dr).rearrange("p (b a) -> p a b", a=2)
                    for par in range(2):
                        ins = dve.tensor_tensor(dm[:, par], dm[:, par], cc[:, par, :].unsqueeze(2).broadcast_to([P, 4, CH]), ALU.add)
                    ins.then_inc(sem("dexp_ready"), 1)
                    dve.wait_ge(sem("d_ready"), i + 1)
                    dve.wait_ge(sem("s_done"), i + 1)
                    dve.tensor_tensor(dmat[:, x_index[u] % 3].rearrange("p h t -> p (h t)"), dmat[:, x_index[u] % 3].rearrange("p h t -> p (h t)"),
                                      bank(0, 1024), ALU.mult).then_inc(sem("sd_ready"), 1)

            def back(u):
                dr, n = units[u]
                if n >= 2:
                    i = x_index[u]
                    dve.wait_ge(sem("num_done"), i + 1)
                    if i >= 1:
                        dve.wait_ge(sem("hs_ready"), i)
                    num = ps[:, 2:4, 0:387].rearrange("p b (j v) -> p b j v", v=P + 1)
                    num2 = ps[:, 4, 0:258].rearrange("p (j v) -> p j v", v=P + 1)
                    chain(dve.tensor_copy(dens[:, 0, 0:6].rearrange("p (b j) -> p b j", j=3), num[:, :, :, P]))
                    chain(dve.tensor_copy(dens[:, 0, 6:8], num2[:, :, P]))
                    own_done()
                    chain(dve.scalar_tensor_tensor(dens[:, 1, :], dens[:, 0, :], -1.0, dens[:, 0, :], ALU.mult, ALU.max))
                    own_done()
                    chain(dve.tensor_tensor(dens[:, 1, :], dens[:, 1, :], col(n, 2, dr), ALU.max))
                    own_done()
                    chain(dve.reciprocal(dens[:, 2, :], dens[:, 1, :]))
                    own_done()
                    if u in sec_index:
                        si = sec_index[u]
                        if si >= 2:
                            dve.wait_ge(sem("turned"), si - 1)
                        dst = tmp[:, si % 2, :]
                    else:
                        dst = hs[:, n - 2, :]
                    dst = dst.rearrange("p (h v) -> p h v", v=P)
                    for b_ in range(2):
                        dve.tensor_tensor(dst[:, 3 * b_:3 * b_ + 3, :], num[:, b_, :, 0:P],
                                          dens[:, 2, 3 * b_:3 * b_ + 3].unsqueeze(2).broadcast_to([P, 3, P]), ALU.mult)
                    dve.tensor_tensor(dst[:, 6:8, :], num2[:, :, 0:P], dens[:, 2, 6:8].unsqueeze(2).broadcast_to([P, 2, P]), ALU.mult)\
                        .then_inc(sem("hs_ready"), 1)
                dve.wait_ge(sem("unit_done"), u + 1)
                if u >= 2:
                    dve.wait_ge(sem("state_ready"), 8 * (u - 1))
                for h in range(HEADS):
                    pair, par = h // 2, h % 2
                    r = slice(64 * par, 64 * par + 64)
                    dve.scalar_tensor_tensor(state[r, dr, h, :], state[r, dr, h, :], alpha[r, dr, pair, n:n + 1],
                                             ps[r, 6 + pair // 3, (P + 1) * (pair % 3):(P + 1) * (pair % 3 + 1)], ALU.mult, ALU.add)\
                        .then_inc(sem("state_ready"), 1)

            def turned(u):
                if u in sec_index:
                    i, c = sec_index[u], units[u][1] - 2
                    dve.wait_ge(sem("ghi_ready"), i + 1)
                    dve.tensor_tensor(g_lo[:, c].rearrange("p h t -> p (h t)"), bank(0, 1024),
                                      g_hi[:, c].rearrange("p h t -> p (h t)").bitcast(F32), ALU.subtract).then_inc(sem("glo_ready"), 1)

            front(0)
            for u in range(len(units)):
                if u + 1 < len(units):
                    front(u + 1)
                back(u)
                if u >= 1:
                    turned(u - 1)
            turned(len(units) - 1)
            for t in range(3):
                lo_tile(K_MOUT + t)
                for d in range(KT):
                    dve.wait_ge(sem("mo_part"), 8 * t + d + 1)
                    dve.wait_ge(sem("y_added"), 8 * (2 * FT + t) + d + 1)
                    b_ = bank(4 + 2 * (d % 2), TX)
                    ins = dve.tensor_copy(y_x[:, d, :], b_) if t == 0 else dve.tensor_tensor(y_x[:, d, :], y_x[:, d, :], b_, ALU.add)
                    ins.then_inc(sem("y_added"), 1)
            post("x_mlstm", "x", 1, 1, y_x, res_x, y_x, lambda: dve.wait_ge(sem("res_in"), 32))
            pre("x_pre2b", "x", 1, 2, y_x, hx_hi, hx_lo, ("x_out", 48 * KT))
            ffn(p2, y_x)
            post("x_out", "x", 1, 3, y_x, res_x, y_x, lambda: dve.wait_ge(sem("res_in"), 48))

        @block.gpsimd
        def _(pool):
            def lo_in(count, slot):
                pool.wait_ge(sem("hi_done"), count)
                pool.tensor_tensor(w_lo[:, slot, 0:2048], raw[:, slot, 0:2048], w_hi[:, slot, 0:2048].bitcast(F32), ALU.subtract)\
                    .then_inc(sem("lo_in"), 1)

            def lo_tile(K):
                lo_in(2 * K + 1, K % 2)

            def ffn(p):
                def tile(j, par, last=False):
                    if not last:
                        lo_in(j * 2 + (2 * p.k0 + 3), (p.k0 + par + 1) % 2)
                    pool.wait_ge(sem("a_hi_ready"), j + (p.j0 + 1))
                    pool.tensor_tensor(a_lo[:, par, 0:p.T], prod[:, 0:p.T], a_hi[:, par, 0:p.T].bitcast(F32), ALU.subtract)\
                        .then_inc(sem("a_lo_ready"), 1)

                tile(0, 0)
                with pool.Fori(0, FT // 2 - 1) as i:
                    tile(i * 2 + 1, 1)
                    tile(i * 2 + 2, 0)
                tile(FT - 1, 1, True)

            def clear(p, y, free):
                free()
                pool.memset(y[:], 0.0).then_inc(sem("y_zero"), 1)

            p0, p1, p2 = PASSES
            lo_tile(p0.k0)
            clear(p0, y_x, lambda: pool.wait_ge(sem("pre_lo"), 8))
            ffn(p0)
            lo_tile(p1.k0)
            for k in range(KT):
                pool.wait_ge(sem("hc_hi"), k + 1)
                pool.tensor_tensor(hc_lo[:, k, :], res_c[:, k, :], hc_hi[:, k, :].bitcast(F32), ALU.subtract).then_inc(sem("hc_split"), 1)
            clear(p1, y_c, lambda: None)
            ffn(p1)
            for t in range(9):
                lo_tile(K_MIN + t)
            for u, (dr, n) in enumerate(units):
                if n >= 2:
                    i = x_index[u]
                    if i == 0:
                        pool.wait_ge(sem("mask_in"), 16)
                    pool.wait_ge(sem(f"row_in{i % 3}"), 64 * (i // 3 + 1))
                    pool.tensor_tensor(dmat[:, x_index[u] % 3], dmat[:, x_index[u] % 3], masks[:, dr, :].unsqueeze(1).broadcast_to([P, HEADS, CH]), ALU.add)\
                        .then_inc(sem("masked"), 1)
                    pool.tensor_tensor(qa[:, x_index[u] % 3], qa[:, x_index[u] % 3], q_x[:, :, (n - 2) * CH:(n - 1) * CH], ALU.mult)\
                        .then_inc(sem("qa_ready"), 1)
                for v in ([u - 2] if u < len(units) - 1 else [u - 2, u - 1, u]):
                    if v in sec_index:
                        i = sec_index[v]
                        c = units[v][1] - 2
                        pool.wait_ge(sem("hs_ready"), x_index[v] + 1)
                        pool.tensor_tensor(tmp[:, i % 2, :], tmp[:, i % 2, :], hs[:, c, :], ALU.add).then_inc(sem("both"), 1)
                        pool.wait_ge(sem("both"), i + 1)
                        pool.wait_ge(sem(f"o_in{i % 2}"), 16 * (i // 2 + 1))
                        pool.tensor_tensor(tmp[:, i % 2, :], tmp[:, i % 2, :], och[:, i % 2, :], ALU.mult).then_inc(sem("gated"), 1)
            for t in range(3):
                lo_tile(K_MOUT + t)
            lo_tile(p2.k0)
            clear(p2, y_x, lambda: pool.wait_ge(sem("pre_lo"), 8 * splits["x_pre2b"] + 8))
            ffn(p2)


_INS = ["x", "ctx", "ccol", "prm", "fcv", "ident", "fold", "inv_x", "inv_c", "pool_w", "modw", "modw1", "ffn_w", "mlstm_w", "masks"]


def lay_out(x, c, ctx, c_ctx, mod_w, mod_b, norm_g, pool_w, pool_scale, mlstm_w_in, mlstm_b_gate,
            mlstm_conv_w, mlstm_conv_b, mlstm_w_out, ffn_w_in, ffn_conv_w, ffn_conv_b, ffn_w_out):
    f = np.float32

    def cols(v):
        return np.asarray(v).reshape(-1, P).T

    def act(v):
        return np.ascontiguousarray(np.asarray(v).T.reshape(KT, P, -1).transpose(1, 0, 2))

    def conv(w, b):
        both = np.concatenate([np.asarray(w).reshape(9, -1), np.asarray(b)[None]], 0)
        return both.reshape(10, -1, P).transpose(2, 1, 0)

    a = {"x": act(x[0]), "ctx": act(ctx[0])}
    a["ccol"] = np.ascontiguousarray(np.stack([cols(c[0]), cols(c_ctx)], -1))
    gate_cols = np.concatenate([np.arange(8) + 32 * i for i in range(4)])
    gb = np.zeros((P,), f)
    gb[gate_cols] = np.asarray(mlstm_b_gate)[0]
    a["prm"] = np.ascontiguousarray(np.concatenate(
        [cols(mod_b[0]), cols(mod_b[1]), cols(np.asarray(norm_g).reshape(-1)), cols(pool_scale[0]),
         conv(mlstm_conv_w[0], mlstm_conv_b[0]).reshape(P, -1), gb[:, None], np.full((P, 1), EPS, f)], 1))
    assert a["prm"].shape[1] == N_PRM
    a["fcv"] = np.ascontiguousarray(np.concatenate([conv(ffn_conv_w[l], ffn_conv_b[l]) for l in range(2)], 1))
    a["ident"] = np.eye(P, dtype=f)
    a["fold"] = np.ascontiguousarray(np.tile(np.eye(32, 2, dtype=f), (4, 1)))
    for name, W in (("inv_x", 64), ("inv_c", 256)):
        pos = np.arange(W)
        inv = [1.0 / (np.clip(pos - w // 2 + w, 0, W) - np.clip(pos - w // 2, 0, W)) for w in WINDOWS]
        a[name] = np.ascontiguousarray(np.broadcast_to(np.stack(inv).astype(f), (P, 4, W)))
    a["pool_w"] = np.ascontiguousarray(np.asarray(pool_w)[0].reshape(4, 2, P, 256).transpose(2, 0, 1, 3))
    a["modw"] = np.ascontiguousarray(
        np.asarray(mod_w)[0].reshape(KT, P, 3, 2048).transpose(2, 0, 1, 3).reshape(24, P, 2048))
    a["modw1"] = np.ascontiguousarray(np.asarray(mod_w)[1].reshape(KT, P, MODC, 512).transpose(2, 1, 0, 3))
    w_in = np.asarray(ffn_w_in).reshape(2, KT, P, 2, FT, P).transpose(0, 4, 2, 3, 1, 5)
    w_out = np.asarray(ffn_w_out).reshape(2, FT, P, D)
    a["ffn_w"] = np.concatenate([w_in[:, :, :, 1].reshape(2, FT, P, D), w_in[:, :, :, 0].reshape(2, FT, P, D), w_out], -1)\
        .reshape(2 * FT, P, WT)
    wm = np.asarray(mlstm_w_in)[0]
    tiles = list(wm[:, :WT].reshape(KT, P, 8, 384).transpose(2, 1, 0, 3).reshape(8, P, WT))
    gate = np.zeros((P, WT), f)
    gate[:, :1024].reshape(P, KT, P)[:, :, gate_cols] = wm[:, WT:].reshape(KT, P, 32).transpose(1, 0, 2)
    wo = np.zeros((9, P, D), f)
    wo[:8] = np.asarray(mlstm_w_out)[0].reshape(8, P, D)
    a["mlstm_w"] = np.ascontiguousarray(np.stack(tiles + [gate] + list(wo.reshape(3, 3, P, D).transpose(0, 2, 1, 3).reshape(3, P, WT))))
    s, t = np.arange(CH)[:, None], np.arange(CH)[None]
    a["masks"] = np.ascontiguousarray(np.stack([np.where(s <= t, 0.0, MASKED), np.where(s >= t, 0.0, MASKED)], 1).astype(f))
    return a


def kernel(**inputs):
    import concourse.bacc as _bacc
    from concourse.bass_utils import run_bass_kernel_spmd as _run

    arrays = lay_out(**inputs)
    nc = _bacc.Bacc("TRN2", target_bir_lowering=False, num_devices=1)
    args = {n: nc.dram_tensor(f"in_{n}", arrays[n].shape, F32, kind="ExternalInput").ap() for n in _INS}
    args["out"] = nc.dram_tensor("out_x", (P, KT, TX), F32, kind="ExternalOutput").ap()
    build(nc, args)
    r = _run(nc, [{f"in_{n}": arrays[n] for n in _INS}], core_ids=[0])
    out = r.results[0]["out_x"]
    return out.transpose(1, 0, 2).reshape(D, TX).T.reshape(1, TX, D)
```
